# Optimizing a Trainium2 kernel written in Bass

```python
import jax, jax.numpy as jnp
from jax import lax
import numpy as np

D_MODEL = 1024
BATCH = 1
SEQ = 1024
DEPTH = 1

CONV_WIDTH = 3
D_CONV = D_MODEL
CONV_GROUPS = 16
RET_HEADS = 4
RET_QK_DIM = D_MODEL // RET_HEADS
RET_V_DIM = 2 * D_MODEL // RET_HEADS
D_RET_QK = RET_HEADS * RET_QK_DIM
D_RET_V = RET_HEADS * RET_V_DIM
CHUNK = 128
ROPE_BASE = 10000.0
EPS = 1e-6
SPLITS = (D_CONV, D_CONV, D_CONV, D_CONV, D_RET_QK, D_RET_QK, D_RET_V, D_RET_V, D_MODEL, D_MODEL)
D_IN = sum(SPLITS)

kernel_name = "hybrid_shortconv_retention_gated_merge"

def rmsnorm(x, g):
    xf = x.astype(jnp.float32)
    y = xf * lax.rsqrt(jnp.mean(xf * xf, axis=-1, keepdims=True) + EPS)
    return (y * g.astype(jnp.float32)).astype(x.dtype)

def short_conv_branch(b_gate, c_gate, xv, z, conv_w, conv_b, w_out):
    u = c_gate * xv
    u = lax.conv_general_dilated(
        u, conv_w[:, None, :],
        window_strides=(1,), padding=[(CONV_WIDTH - 1, 0)],
        dimension_numbers=('NWC', 'WIO', 'NWC'),
        feature_group_count=D_CONV) + conv_b
    y = b_gate * u * jax.nn.silu(z)
    return y @ w_out

def rotary(t, cos, sin):
    t1, t2 = jnp.split(t, 2, axis=-1)
    c = cos[None, :, None, :]
    s = sin[None, :, None, :]
    return jnp.concatenate([t1 * c - t2 * s, t1 * s + t2 * c], axis=-1)

def retention_branch(q, k, v, z, w_out):
    bsz, seq, _ = q.shape
    n_chunks = seq // CHUNK
    f32 = jnp.float32
    q = q.reshape(bsz, seq, RET_HEADS, RET_QK_DIM).astype(f32)
    k = k.reshape(bsz, seq, RET_HEADS, RET_QK_DIM).astype(f32)
    v = v.reshape(bsz, seq, RET_HEADS, RET_V_DIM).astype(f32)

    pos = jnp.arange(seq, dtype=f32)
    inv_freq = ROPE_BASE ** (-jnp.arange(0, RET_QK_DIM, 2, dtype=f32) / RET_QK_DIM)
    ang = pos[:, None] * inv_freq[None, :]
    cos, sin = jnp.cos(ang), jnp.sin(ang)
    q = rotary(q, cos, sin)
    k = rotary(k, cos, sin) * (RET_QK_DIM ** -0.5)

    log_gamma = jnp.log(1.0 - jnp.exp2(-5.0 - jnp.arange(RET_HEADS, dtype=f32)))
    idx = jnp.arange(CHUNK, dtype=f32)
    rel = idx[:, None] - idx[None, :]
    decay_in = jnp.where(rel[None] >= 0,
                         jnp.exp(jnp.maximum(rel, 0.0)[None] * log_gamma[:, None, None]),
                         0.0)
    xi = jnp.exp((idx + 1.0)[:, None] * log_gamma[None, :])
    zeta = jnp.exp((CHUNK - 1.0 - idx)[:, None] * log_gamma[None, :])
    chunk_decay = jnp.exp(CHUNK * log_gamma)

    qc = q.reshape(bsz, n_chunks, CHUNK, RET_HEADS, RET_QK_DIM)
    kc = k.reshape(bsz, n_chunks, CHUNK, RET_HEADS, RET_QK_DIM)
    vc = v.reshape(bsz, n_chunks, CHUNK, RET_HEADS, RET_V_DIM)

    s = jnp.einsum('bnihd,bnjhd->bnhij', qc, kc) * decay_in[None, None]
    o_in = jnp.einsum('bnhij,bnjhe->bnihe', s, vc)

    def step(state, inp):
        qn, kn, vn = inp
        cross = jnp.einsum('bihd,bhde->bihe', qn, state) * xi[None, :, :, None]
        state = state * chunk_decay[None, :, None, None] + jnp.einsum(
            'bjhd,bjhe->bhde', kn * zeta[None, :, :, None], vn)
        return state, cross

    s0 = jnp.zeros((bsz, RET_HEADS, RET_QK_DIM, RET_V_DIM), f32)
    _, o_cross = lax.scan(step, s0, (jnp.moveaxis(qc, 1, 0), jnp.moveaxis(kc, 1, 0),
                                     jnp.moveaxis(vc, 1, 0)))
    o = (o_in + jnp.moveaxis(o_cross, 0, 1)).reshape(bsz, seq, RET_HEADS, RET_V_DIM)

    o = o * lax.rsqrt(jnp.mean(o * o, axis=-1, keepdims=True) + EPS)
    o = o.reshape(bsz, seq, D_RET_V).astype(z.dtype) * jax.nn.silu(z)
    return o @ w_out

def setup_inputs(seed: int = 0) -> dict:
    key = jax.random.key(seed)
    ks = jax.random.split(key, 10)
    f32 = jnp.float32
    x = jax.random.normal(ks[0], (BATCH, SEQ, D_MODEL), f32)
    norm_g = 1.0 + 0.01 * jax.random.normal(ks[1], (DEPTH, D_MODEL), f32)
    w_in = jax.random.normal(ks[2], (DEPTH, D_MODEL, D_IN), f32) * D_MODEL ** -0.5
    conv_w = jax.random.normal(ks[3], (DEPTH, CONV_WIDTH, D_CONV), f32) * CONV_WIDTH ** -0.5
    conv_b = 0.01 * jax.random.normal(ks[4], (DEPTH, D_CONV), f32)
    w_a_out = jax.random.normal(ks[5], (DEPTH, D_CONV, D_MODEL), f32) * D_CONV ** -0.5
    w_b_out = jax.random.normal(ks[6], (DEPTH, D_RET_V, D_MODEL), f32) * D_RET_V ** -0.5
    w_o = jax.random.normal(ks[7], (DEPTH, D_MODEL, D_MODEL), f32) * D_MODEL ** -0.5
    final_g = 1.0 + 0.01 * jax.random.normal(ks[8], (D_MODEL,), f32)
    return {"x": x, "norm_g": norm_g, "w_in": w_in, "conv_w": conv_w, "conv_b": conv_b,
            "w_a_out": w_a_out, "w_b_out": w_b_out, "w_o": w_o, "final_g": final_g}

def reference(x, norm_g, w_in, conv_w, conv_b, w_a_out, w_b_out, w_o, final_g):
    split_points = list(np.cumsum(SPLITS)[:-1])
    for layer in range(DEPTH):
        h = rmsnorm(x, norm_g[layer])
        proj = h @ w_in[layer]
        b_a, c_a, x_a, z_a, q, k, v, z_b, g_a, g_b = jnp.split(proj, split_points, axis=-1)
        y_a = short_conv_branch(b_a, c_a, x_a, z_a, conv_w[layer], conv_b[layer], w_a_out[layer])
        y_b = retention_branch(q, k, v, z_b, w_b_out[layer])
        merged = jax.nn.sigmoid(g_a) * y_a + jax.nn.sigmoid(g_b) * y_b
        x = x + merged @ w_o[layer]
    return rmsnorm(x, final_g)


_drawn_inputs = setup_inputs


def setup_inputs(seed=0):
    import zlib

    import numpy as np

    out = dict(_drawn_inputs(seed))
    spreads = {}
    factors = {'norm_g': 6.154, 'conv_b': 200.0, 'final_g': 200.0, 'w_b_out': 8.0}
    for name, (base, spread) in spreads.items():
        noise = np.random.default_rng([zlib.crc32(name.encode()), seed]).standard_normal(out[name].shape)
        drawn = base * np.exp(spread * noise) if base else spread * noise
        out[name] = __import__('jax').numpy.asarray(drawn.astype(out[name].dtype))
    for name, factor in factors.items():
        out[name] = (out[name] * factor).astype(out[name].dtype)
    return out
```

```python
from contextlib import ExitStack

import numpy as np
import concourse.bass as bass
from concourse import mybir

F32 = mybir.dt.float32
F32R = mybir.dt.float32r
BF16 = mybir.dt.bfloat16
ACT = mybir.ActivationFunctionType
ALU = mybir.AluOpType

P = 128
D = 1024
T = 1024
KT = D // P
TT = T // P
BANK = 512
BANKS = 8
BLOCK = 1024
HEADS = 4
QK = D // HEADS
DQ = QK // P
V = 2 * D // HEADS
ET = V // P
CHUNK = P
EPS = 1e-6
HALF = T // 2
CONV = 3
RING = 4
RAW = 2

GB_BLOCKS, SILU_BLOCKS, CONV_BLOCKS, MIX_BLOCKS = KT, 4 * HEADS, 4 * KT, 2 * KT
HEAD_BLOCKS, YB_BLOCKS, OUT_BLOCKS = 8, HEADS * ET, KT
SILU_0 = GB_BLOCKS
CONV_0 = SILU_0 + SILU_BLOCKS
MIX_0 = CONV_0 + CONV_BLOCKS
HEAD_0 = MIX_0 + MIX_BLOCKS
LAST_0 = HEAD_0 + HEADS * HEAD_BLOCKS
HALF_BLOCKS = YB_BLOCKS + OUT_BLOCKS
STREAM = LAST_0 + 2 * HALF_BLOCKS

READ_GB = 1
READ_SILU = READ_GB + GB_BLOCKS // 4
READ_CONV = READ_SILU + 2 * HEADS
READ_MIX = READ_CONV + KT
READ_HEAD = READ_MIX + MIX_BLOCKS // 4
RET_READS = [TT, TT - 1, TT, TT]


def head_read(j, h, n):
    return (3 + RET_READS[j]) * h + (READ_HEAD + n)


def ret_read(j, h, n):
    return head_read(j, h, 3 + n + 1)


def last_read(j, half, n):
    return READ_HEAD + HEADS * (3 + RET_READS[j]) + 3 * half + n


def full_head(bank, h, n):
    uses = [4, 4, TT - 1, TT - 1, 4, 4, 4, 4][bank]
    return uses * h + n if bank == 7 else (1 + uses) * h + (HEADS + n + 1)


def full_last(bank, half, n):
    return full_head(bank, HEADS, 0) + 2 * half + n


def constants():
    freq = (10000.0 ** (-(np.arange(0, QK, 2, dtype=np.float32) / np.float32(QK)).astype(np.float64)))
    freq = freq.astype(np.float32)
    angle = (np.arange(T, dtype=np.float32)[None, :] * freq[:, None]).astype(np.float64)
    rope = np.stack([np.cos(angle), np.sin(angle)]).astype(np.float32)
    table = np.zeros((HEADS, P, P + 4), np.float64)
    j = np.arange(P, dtype=np.float64)
    for h in range(HEADS):
        gamma = 1.0 - 2.0 ** (-5.0 - h)
        xi = gamma ** (j + 1)
        table[h, :, :P] = (j[None, :] >= j[:, None]) * (gamma ** -(j + 1))[:, None] * QK ** -0.5
        table[h, :, P] = gamma ** (CHUNK - 1 - j) * QK ** -0.5
        table[h, :, P + 1] = xi / np.sqrt(V)
        table[h, :, P + 2] = xi
        table[h, :, P + 3] = gamma ** CHUNK
    return rope, table.astype(np.float32), np.eye(P, dtype=np.float32)


def build(nc, x_t, x_rows, columns, weights, final_g, rope, head_table, identity, out):
    gate_b_d = nc.dram_tensor("gate_b_scratch", (KT, P, T), F32, kind="Internal").ap()
    mixed_a_d = nc.dram_tensor("mixed_a_scratch", (KT, P, T), F32, kind="Internal").ap()
    silu_d = nc.dram_tensor("silu_scratch", (HEADS, TT, P, V), F32, kind="Internal").ap()
    o_d = nc.dram_tensor("o_scratch", (2, HEADS * ET, P, HALF), F32, kind="Internal").ap()

    held = ExitStack()

    def sb(stack, name, shape, dt):
        return stack.enter_context(nc.sbuf_tensor(name, shape, dt))

    def sem(name):
        return held.enter_context(nc.semaphore(name))

    w_hi = sb(held, "w_hi", [P, RING, BLOCK], F32R)
    w_lo = sb(held, "w_lo", [P, RING, BLOCK], F32R)
    w_raw = sb(held, "w_raw", [P, RAW, BLOCK], F32)
    ident = sb(held, "ident", [P, P], F32)
    ident_r = sb(held, "ident_r", [P, P], F32R)
    NCOL = KT * (2 + CONV)
    cols = sb(held, "cols", [P, NCOL], F32)
    small = sb(held, "small", [P, 4 * TT + 1], F32)
    rms_var, rms_scale, minus_half = (small[:, n * TT:(n + 1) * TT] for n in range(3))
    square_sum = small[:, 3 * TT:4 * TT]
    eps = small[:, 4 * TT:4 * TT + 1]
    psum = held.enter_context(nc.psum_tensor("psum", [P, BANKS, BANK], F32))

    def g_col(k):
        return cols[:, k:k + 1]

    with ExitStack() as upper:
        h_hi = sb(upper, "h_hi", [P, KT, T], F32R)
        h_lo = sb(upper, "h_lo", [P, KT, T], F32R)
        with ExitStack() as s:
            x_raw = sb(s, "x_raw", [P, KT, T], F32)
            squares = sb(s, "squares", [P, KT, T], F32)
            ones = sb(s, "ones", [P, P], F32)
            diagonal = sb(s, "diagonal", [P, TT, P], F32)
        with ExitStack() as s:
            gate_b = sb(s, "gate_b", [P, 4, T], F32)
            sig_z = sb(s, "sig_z", [P, TT, V], F32)
            silu_z = sb(s, "silu_z", [P, TT, V], F32)
        with ExitStack() as s:
            y_hi = sb(s, "y_hi", [P, KT, T], F32R)
            y_lo = sb(s, "y_lo", [P, KT, T], F32R)
            with ExitStack() as s2:
                u_pad = sb(s2, "u_pad", [P, T + CONV - 1], F32)
                taps = sb(s2, "taps", [P, T], F32)
                gate_zb = sb(s2, "gate_zb", [P, T], F32)
            with ExitStack() as s2:
                sig_a = sb(s2, "sig_a", [P, 2, T], F32)
                mixed_a = sb(s2, "mixed_a", [P, 2, T], F32)
        with ExitStack() as s:
            q_hi = sb(s, "q_hi", [P, DQ, T], F32R)
            q_lo = sb(s, "q_lo", [P, DQ, T], F32R)
            k_hi = sb(s, "k_hi", [P, DQ, T], F32R)
            k_lo = sb(s, "k_lo", [P, DQ, T], F32R)
            v_hi = sb(s, "v_hi", [P, TT, V], F32R)
            v_lo = sb(s, "v_lo", [P, TT, V], F32R)
            state_hi = sb(s, "state_hi", [P, 2, DQ * V], F32R)
            state_lo = sb(s, "state_lo", [P, 2, DQ * V], F32R)
            score_hi = sb(s, "score_hi", [P, 2, P], F32R)
            score_lo = sb(s, "score_lo", [P, 2, P], F32R)
            key_hi = sb(s, "key_hi", [P, 2, QK], F32R)
            key_lo = sb(s, "key_lo", [P, 2, QK], F32R)
            with ExitStack() as s2:
                rope_sb = sb(s2, "rope_sb", [P, 2, T], F32)
                turn_1 = sb(s2, "turn_1", [P, T], F32)
                turn_2 = sb(s2, "turn_2", [P, T], F32)
            with ExitStack() as s2:
                state = sb(s2, "state", [P, DQ * V], F32)
                silu_in = sb(s2, "silu_in", [P, 2, V], F32)
                o_t = sb(s2, "o_t", [P, 2, ET, P], F32)
                o_rows = sb(s2, "o_rows", [P, V], F32)
                table = sb(s2, "table", [P, P + 4], F32)
                unused = sb(s2, "unused", [P, V], BF16)
    with ExitStack() as last:
        o_raw = sb(last, "o_raw", [P, RING, HALF], F32)
        o_hi = sb(last, "o_hi", [P, RING, HALF], F32R)
        o_lo = sb(last, "o_lo", [P, RING, HALF], F32R)
        m_hi = sb(last, "m_hi", [P, KT, HALF], F32R)
        m_lo = sb(last, "m_lo", [P, KT, HALF], F32R)
        merged = sb(last, "merged", [P, KT, HALF], F32)
        gate_b_in = sb(last, "gate_b_in", [P, KT, HALF], F32)
        mixed_in = sb(last, "mixed_in", [P, KT, HALF], F32)
        result = sb(last, "result", [P, 4, D], F32)
        final_sb = sb(last, "final_sb", [P, D], F32)
        unused_last = sb(last, "unused_last", [P, D], BF16)

    decay, key_decay, xi_mean, xi, chunk_decay = (
        table[:, 0:P], table[:, P:P + 1], table[:, P + 1:P + 2], table[:, P + 2:P + 3], table[:, P + 3:P + 4])

    raw_in = [sem(f"raw_in{n}") for n in range(RAW)]
    hi_ready = sem("hi_ready")
    parts_ready = sem("parts_ready")
    block_done = sem("block_done")
    bank_full = [sem(f"bank_full{b}") for b in range(BANKS)]
    pair_read = [sem(f"pair_read{j}") for j in range(BANKS // 2)]
    consts_in = sem("consts_in")
    x_in = [sem(f"x_in{k}") for k in range(KT)]
    pool_consts = sem("pool_consts")
    ident_ready = sem("ident_ready")
    squares_ready = sem("squares_ready")
    sums_full = sem("sums_full")
    rms_ready = sem("rms_ready")
    diag_ready = sem("diag_ready")
    rms_full = sem("rms_full")
    h_scaled = sem("h_scaled")
    h_hi_ready = sem("h_hi_ready")
    h_ready = sem("h_ready")
    gate_b_out = sem("gate_b_out")
    sig_z_ready = sem("sig_z_ready")
    silu_out = sem("silu_out")
    sig_c_ready = sem("sig_c_ready")
    conv_step = sem("conv_step")
    y_ready = sem("y_ready")
    mixed_out = sem("mixed_out")
    rope_in = sem("rope_in")
    turn_step = sem("turn_step")
    turn_hi_ready = sem("turn_hi_ready")
    v_hi_ready = sem("v_hi_ready")
    table_in = sem("table_in")
    silu_back = [sem(f"silu_back{n}") for n in range(2)]
    score_made = sem("score_made")
    score_hi_ready = sem("score_hi_ready")
    state_hi_ready = sem("state_hi_ready")
    state_ready = sem("state_ready")
    o_square_ready = sem("o_square_ready")
    o_var_ready = sem("o_var_ready")
    o_scale_ready = sem("o_scale_ready")
    o_out = [sem(f"o_out{n}") for n in range(2)]
    o_back = [sem(f"o_back{n}") for n in range(RING)]
    o_hi_ready = sem("o_hi_ready")
    o_ready = sem("o_ready")
    gates_back = sem("gates_back")
    merged_ready = sem("merged_ready")
    m_hi_ready = sem("m_hi_ready")
    m_ready = sem("m_ready")
    result_in = sem("result_in")
    final_in = sem("final_in")
    last_square_ready = sem("last_square_ready")
    last_var_ready = sem("last_var_ready")
    last_scale_ready = sem("last_scale_ready")
    result_ready = sem("result_ready")
    result_out = sem("result_out")

    CONV_STEPS, TURN_STEPS = 5, 6
    OUT_TILES = HALF // P

    def pair(j):
        return psum[:, 2 * j:2 * j + 2, :].rearrange("p b n -> p (b n)")

    block = held.enter_context(nc.Block())

    @block.sync
    def _(sp):
        def load_block(b, offset):
            n = offset + RAW + 2
            sp.wait_ge(parts_ready, b + (n - RAW + 1))
            sp.dma_start(w_raw[:, n % RAW, :], weights[b + n]).then_inc(raw_in[n % RAW], 16)

        sp.sem_inc(gate_b_out, 4 * 16)
        sp.sem_inc(silu_out, TT * 16)
        sp.sem_inc(mixed_out, 2 * 16)
        for n in range(2):
            sp.sem_inc(o_out[n], 16)

        sp.dma_start(x_raw[:, 0, :], x_t[0]).then_inc(x_in[0], 16)
        sp.dma_start(ident[:, :], identity).then_inc(consts_in, 16)
        sp.dma_start(cols[:, :], columns).then_inc(consts_in, 16)
        for k in range(1, KT):
            sp.dma_start(x_raw[:, k, :], x_t[k]).then_inc(x_in[k], 16)
        for n in range(RAW):
            sp.dma_start(w_raw[:, n, :], weights[n]).then_inc(raw_in[n], 16)
        for n in range(2):
            load_block(0, n - 2)

        with sp.Fori(0, GB_BLOCKS // 4) as i:
            for j in range(4):
                load_block(4 * i, j)
                sp.wait_ge(pair_read[j], i + (READ_GB + 1))
                sp.dma_start(gate_b_d[4 * i + j], gate_b[:, j, :]).then_inc(gate_b_out, 16)

        with sp.Fori(0, HEADS) as g:
            for s in range(4):
                load_block(4 * g, SILU_0 + s)
            for t in range(TT):
                sp.wait_ge(pair_read[t // 2], 2 * g + (READ_SILU + t % 2 + 1))
                sp.dma_start(silu_d[g, t], silu_z[:, t, :]).then_inc(silu_out, 16)

        with sp.Fori(0, KT) as c:
            for j in range(4):
                load_block(4 * c, CONV_0 + j)

        with sp.Fori(0, KT // 2) as i:
            for j in range(4):
                load_block(4 * i, MIX_0 + j)
                if j % 2:
                    sp.wait_ge(pair_read[j], i + (READ_MIX + 1))
                    sp.dma_start(mixed_a_d[2 * i + j // 2], mixed_a[:, j // 2, :]).then_inc(mixed_out, 16)

        with sp.Fori(0, HEADS) as h:
            for n in range(2):
                sp.wait_ge(o_out[n], 64 * h + 16)
            sp.wait_ge(mixed_out, (2 + KT) * 16)
            sp.dma_start(rope_sb[:, :, :], rope.rearrange("c p t -> p c t")).then_inc(rope_in, 16)
            for j in range(HEAD_BLOCKS):
                load_block(HEAD_BLOCKS * h, HEAD_0 + j)
                if j == 5:
                    sp.wait_ge(turn_step, 2 * TURN_STEPS * h + 3 * TURN_STEPS)
                    sp.wait_ge(turn_hi_ready, 4 * h + 4)
                    sp.dma_start(table[:, :], head_table[h]).then_inc(table_in, 16)
                    for n in range(2):
                        sp.dma_start(silu_in[:, n, :], silu_d[h, n]).then_inc(silu_back[n], 16)
            for n in range(TT):
                if n + 2 < TT:
                    sp.wait_ge(pair_read[2], ret_read(2, h, n))
                    sp.dma_start(silu_in[:, n % 2, :], silu_d[h, n + 2]).then_inc(silu_back[n % 2], 16)
                sp.wait_ge(pair_read[3], ret_read(3, h, n))
                at = (n % 4) * P
                sp.dma_start(o_d[n // 4].rearrange("(h e) p c -> h p e c", e=ET)[h, :, :, at:at + P],
                             o_t[:, n % 2, :, :]).then_inc(o_out[n % 2], 16)

        def load_o(half, e):
            sp.dma_start(o_raw[:, e % RING, :], o_d[half, e]).then_inc(o_back[e % RING], 16)

        for n in range(2):
            sp.wait_ge(o_out[n], 64 * HEADS + 16)
        for e in range(RING):
            load_o(0, e)
        for half in range(2):
            first = LAST_0 + half * HALF_BLOCKS
            at = half * HALF
            if half:
                sp.wait_ge(merged_ready, half * KT)
            sp.dma_start(gate_b_in[:, :, :], gate_b_d[:, :, at:at + HALF].rearrange("k p t -> p k t"))\
                .then_inc(gates_back, 16)
            sp.dma_start(mixed_in[:, :, :], mixed_a_d[:, :, at:at + HALF].rearrange("k p t -> p k t"))\
                .then_inc(gates_back, 16)
            if half == 0:
                sp.dma_start(final_sb[:, :], final_g).then_inc(final_in, 16)
            with sp.Fori(0, YB_BLOCKS // RING - 1) as i:
                for j in range(RING):
                    load_block(4 * i, first + j)
                    sp.wait_ge(o_ready, 4 * i + (half * YB_BLOCKS + j + 1))
                    sp.dma_start(o_raw[:, j, :], o_d[half, 4 * i + (j + RING)]).then_inc(o_back[j], 16)
            for j in range(RING):
                load_block(0, first + YB_BLOCKS - RING + j)
            if half:
                sp.wait_ge(result_out, 16 * OUT_TILES)
            sp.dma_start(result[:, :, :], x_rows[half * OUT_TILES:(half + 1) * OUT_TILES].rearrange("t p n -> p t n"))\
                .then_inc(result_in, 16)
            for k in range(OUT_BLOCKS):
                if first + YB_BLOCKS + k + RAW + 2 < STREAM:
                    load_block(0, first + YB_BLOCKS + k)
                if half == 0 and k < RING:
                    sp.wait_ge(o_ready, YB_BLOCKS - RING + k + 1)
                    load_o(1, k)
            for t in range(OUT_TILES):
                sp.wait_ge(result_ready, half * OUT_TILES + t + 1)
                sp.dma_start(out[half * OUT_TILES + t], result[:, t, :]).then_inc(result_out, 16)
        sp.wait_ge(result_out, 2 * OUT_TILES * 16)

    @block.gpsimd
    def _(pool):
        pool.memset(ones[:, :], 1.0).then_inc(pool_consts, 1)
        pool.memset(minus_half, -0.5).then_inc(pool_consts, 1)
        pool.memset(eps, EPS).then_inc(pool_consts, 1)
        pool.wait_ge(pool_consts, 3)
        pool.wait_ge(pair_read[2], READ_GB)
        nc.gpsimd.tensor_tensor(rms_scale, rms_var, minus_half, ALU.pow).then_inc(rms_ready, 1)
        for k in range(KT):
            pool.wait_ge(h_hi_ready, k + 1)
            nc.gpsimd.tensor_tensor(h_lo[:, k, :], x_raw[:, k, :], h_hi[:, k, :].bitcast(F32), ALU.subtract)\
                .then_inc(h_ready, 1)

        def o_factor(h, n):
            v = rms_var[:, n % 2:n % 2 + 1]
            r = rms_scale[:, n % 2:n % 2 + 1]
            pool.wait_ge(o_square_ready, TT * h + (n + 1))
            nc.gpsimd.tensor_tensor(v, square_sum[:, n % 2:n % 2 + 1], eps, ALU.add)\
                .then_inc(o_var_ready, 1)
            pool.wait_ge(o_var_ready, 2 * TT * h + (2 * n + 1))
            nc.gpsimd.tensor_tensor(r, v, minus_half[:, 0:1], ALU.pow).then_inc(o_var_ready, 1)
            pool.wait_ge(o_var_ready, 2 * TT * h + (2 * n + 2))
            nc.gpsimd.tensor_tensor(r, r, xi, ALU.mult).then_inc(o_scale_ready, 1)

        def state_low(h, n):
            pool.wait_ge(state_hi_ready, (TT - 1) * h + (n + 1))
            nc.gpsimd.tensor_tensor(state_lo[:, n % 2, :], state[:, :], state_hi[:, n % 2, :].bitcast(F32),
                                    ALU.subtract).then_inc(state_ready, 1)

        with pool.Fori(0, HEADS) as h:
            pool.wait_ge(table_in, 16 * h + 16)
            state_low(h, 0)
            for n in range(TT):
                o_factor(h, n)
                if n + 1 < TT - 1:
                    state_low(h, n + 1)

        for t in range(2 * OUT_TILES):
            v, r = rms_var[:, t % 2:t % 2 + 1], rms_scale[:, t % 2:t % 2 + 1]
            pool.wait_ge(last_square_ready, t + 1)
            nc.gpsimd.tensor_scalar(v, square_sum[:, t % 2:t % 2 + 1], 1.0 / D, EPS, ALU.mult, ALU.add)\
                .then_inc(last_var_ready, 1)
            pool.wait_ge(last_var_ready, t + 1)
            nc.gpsimd.tensor_tensor(r, v, minus_half[:, 0:1], ALU.pow).then_inc(last_scale_ready, 1)

    @block.scalar
    def _(act):
        def split_hi(b, offset):
            n = offset
            act.wait_ge(raw_in[n % RAW], 8 * b + 16 * (n // RAW + 1))
            act.wait_ge(block_done, b + (n + 1))
            nc.scalar.activation(w_hi[:, n % RING, :], w_raw[:, n % RAW, :], ACT.Copy).then_inc(hi_ready, 1)

        for k in range(KT):
            act.wait_ge(x_in[k], 16)
            nc.scalar.activation(squares[:, k, :], x_raw[:, k, :], ACT.Square).then_inc(squares_ready, 1)
        act.wait_ge(consts_in, 32)
        nc.scalar.activation(ident_r[:, :], ident[:, :], ACT.Copy).then_inc(ident_ready, 1)
        split_hi(0, 0)
        split_hi(0, 1)
        for k in range(KT):
            act.wait_ge(h_scaled, k + 1)
            nc.scalar.activation(h_hi[:, k, :], x_raw[:, k, :], ACT.Copy).then_inc(h_hi_ready, 1)

        act.wait_ge(h_ready, KT)
        with act.Fori(0, GB_BLOCKS // 4) as i:
            for j in range(4):
                split_hi(4 * i, j + 2)
                act.wait_ge(block_done, 4 * i + (RING + j + 1))
                act.wait_ge(gate_b_out, 64 * i + 64)
                nc.scalar.activation(gate_b[:, j, :], pair(j), ACT.Sigmoid).then_inc(pair_read[j], 1)

        with act.Fori(0, HEADS) as g:
            for s in range(4):
                split_hi(4 * g, SILU_0 + s + 2)
            for t in range(TT):
                if t < BANKS - 1:
                    act.wait_ge(bank_full[t], g + 1)
                else:
                    act.wait_ge(block_done, 4 * g + (RING + SILU_0 + 4))
                nc.scalar.activation(sig_z[:, t, :], psum[:, t, :], ACT.Sigmoid).then_inc(sig_z_ready, 1)

        with act.Fori(0, KT) as c:
            split_hi(4 * c, CONV_0 + 2)
            act.wait_ge(block_done, 4 * c + (RING + CONV_0 + 1))
            act.wait_ge(conv_step, CONV_STEPS * c + 3)
            nc.scalar.activation(u_pad[:, CONV - 1:], pair(0), ACT.Copy).then_inc(pair_read[0], 1)
            split_hi(4 * c, CONV_0 + 3)
            split_hi(4 * c, CONV_0 + 4)
            act.wait_ge(block_done, 4 * c + (RING + CONV_0 + 3))
            act.wait_ge(conv_step, CONV_STEPS * c + 4)
            nc.scalar.activation(gate_zb[:, :], pair(2), ACT.Sigmoid).then_inc(sig_c_ready, 1)
            split_hi(4 * c, CONV_0 + 5)

        act.wait_ge(y_ready, KT)
        with act.Fori(0, KT // 2) as i:
            for j in (0, 2):
                split_hi(4 * i, MIX_0 + j + 2)
                act.wait_ge(block_done, 4 * i + (RING + MIX_0 + j + 1))
                act.wait_ge(pair_read[j + 1], i + READ_MIX)
                nc.scalar.activation(sig_a[:, j // 2, :], pair(j), ACT.Sigmoid).then_inc(pair_read[j], 1)
                split_hi(4 * i, MIX_0 + j + 3)

        def score_parts(h, n):
            act.wait_ge(score_made, TT * h + (n + 1))
            if n >= 2:
                act.wait_ge(bank_full[4 + n % 2], full_head(4, h, 1 + (n - 2) // 2))
            nc.scalar.activation(score_hi[:, n % 2, :], psum[:, n % 2, 0:P], ACT.Copy).then_inc(score_hi_ready, 1)
            if n < TT - 1:
                nc.scalar.activation(key_hi[:, n % 2, :], psum[:, n % 2, P:P + QK], ACT.Copy)\
                    .then_inc(score_hi_ready, 1)

        def state_parts(h, n):
            act.wait_ge(pair_read[1], ret_read(1, h, n))
            if n >= 2:
                act.wait_ge(bank_full[4 + (n - 1) % 2], full_head(4, h, 1 + (n - 1) // 2))
            nc.scalar.activation(state_hi[:, n % 2, :], state[:, :], ACT.Copy).then_inc(state_hi_ready, 1)

        def o_back_copy(h, n):
            act.wait_ge(bank_full[6 + n % 2], full_head(6 + n % 2, h, 1 + n // 2))
            act.wait_ge(o_out[n % 2], 64 * h + 16 * (n // 2 + 1))
            nc.scalar.activation(o_t[:, n % 2, :, :].rearrange("p e c -> p (e c)"), psum[:, 6 + n % 2, :], ACT.Copy)\
                .then_inc(pair_read[3], 1)

        with act.Fori(0, HEADS) as h:
            for j in range(4):
                split_hi(HEAD_BLOCKS * h, HEAD_0 + j + 2)
                if j % 2:
                    for d, part in enumerate((turn_1, turn_2)):
                        dst = (q_hi, k_hi)[j // 2]
                        act.wait_ge(turn_step, 2 * TURN_STEPS * h + (TURN_STEPS * (1 + j // 2) + (3, 5)[d]))
                        nc.scalar.activation(dst[:, d, :], part[:, :], ACT.Copy).then_inc(turn_hi_ready, 1)
            for s in range(4):
                split_hi(HEAD_BLOCKS * h, HEAD_0 + 4 + s + 2)
            for t in range(TT):
                if t < BANKS - 1:
                    act.wait_ge(bank_full[t], full_head(t, h, 0))
                else:
                    act.wait_ge(block_done, HEAD_BLOCKS * h + (RING + HEAD_0 + HEAD_BLOCKS))
                nc.scalar.activation(v_hi[:, t, :], psum[:, t, :], ACT.Copy).then_inc(v_hi_ready, 1)
            score_parts(h, 0)
            score_parts(h, 1)
            state_parts(h, 0)
            act.wait_ge(table_in, 16 * h + 16)
            for n in range(TT):
                if n + 2 < TT:
                    score_parts(h, n + 2)
                act.wait_ge(bank_full[4 + n % 2], full_head(4, h, 1 + n // 2))
                if n:
                    act.wait_ge(o_square_ready, TT * h + n)
                nc.scalar.activation(unused[:, :], psum[:, 4 + n % 2, :], ACT.Square,
                                     scale=xi_mean, accum_out=square_sum[:, n % 2:n % 2 + 1])\
                    .then_inc(o_square_ready, 1)
                if n + 1 < TT - 1:
                    state_parts(h, n + 1)
                if n:
                    o_back_copy(h, n - 1)
            o_back_copy(h, TT - 1)

        def split_o_hi(i, e):
            act.wait_ge(o_back[e % RING], 16 * i + 16 * (e // RING + 1))
            if e >= RING:
                half, tile = divmod(e - RING, YB_BLOCKS)
                act.wait_ge(block_done, 4 * i + (RING + LAST_0 + half * HALF_BLOCKS + tile + 1))
            nc.scalar.activation(o_hi[:, e % RING, :], o_raw[:, e % RING, :], ACT.Copy).then_inc(o_hi_ready, 1)

        split_o_hi(0, 0)
        split_o_hi(0, 1)
        for half in range(2):
            first, e0 = LAST_0 + half * HALF_BLOCKS, half * YB_BLOCKS
            for j in range(2):
                split_hi(0, first + j + 2)
                split_o_hi(0, e0 + j + 2)
            with act.Fori(0, YB_BLOCKS // RING - 1) as i:
                for j in range(2, 2 + RING):
                    split_hi(4 * i, first + j + 2)
                    split_o_hi(i, e0 + j + 2)
            for j in range(YB_BLOCKS - 2, YB_BLOCKS):
                split_hi(0, first + j + 2)
            for k in range(KT):
                act.wait_ge(merged_ready, half * KT + k + 1)
                if half and k == 0:
                    act.wait_ge(block_done, RING + LAST_0 + HALF_BLOCKS)
                nc.scalar.activation(m_hi[:, k, :], merged[:, k, :], ACT.Copy).then_inc(m_hi_ready, 1)
                if first + YB_BLOCKS + k + 2 < STREAM:
                    split_hi(0, first + YB_BLOCKS + k + 2)
                if half == 0 and k >= OUT_BLOCKS - 2:
                    split_o_hi(0, YB_BLOCKS + k - (OUT_BLOCKS - 2))
            for t in range(OUT_TILES):
                act.wait_ge(pair_read[t], last_read(t, half, 3))
                if half or t:
                    act.wait_ge(last_square_ready, half * OUT_TILES + t)
                nc.scalar.activation(unused_last[:, :], result[:, t, :], ACT.Square,
                                     accum_out=square_sum[:, t % 2:t % 2 + 1]).then_inc(last_square_ready, 1)

    @block.vector
    def _(dve):
        def split_lo(b, offset):
            n = offset
            dve.wait_ge(hi_ready, b + (n + 1))
            nc.vector.tensor_tensor(w_lo[:, n % RING, :], w_raw[:, n % RAW, :], w_hi[:, n % RING, :].bitcast(F32),
                                    ALU.subtract).then_inc(parts_ready, 1)

        for j in (0, 1, 3):
            dve.sem_inc(pair_read[j], 1)
        dve.sem_inc(conv_step, CONV_STEPS)
        dve.sem_inc(turn_step, TURN_STEPS)

        split_lo(0, 0)
        split_lo(0, 1)
        dve.wait_ge(sums_full, 1)
        nc.vector.tensor_scalar(rms_var, psum[:, 5, 0:TT], 1.0 / D, EPS, ALU.mult, ALU.add)\
            .then_inc(pair_read[2], 1)
        dve.wait_ge(rms_ready, 1)
        dve.wait_ge(consts_in, 32)
        for t in range(TT):
            nc.vector.tensor_scalar(diagonal[:, t, :], ident[:, :], rms_scale[:, t:t + 1], None, ALU.mult)\
                .then_inc(diag_ready, 1)
        dve.wait_ge(rms_full, 2)
        for k in range(KT):
            nc.vector.scalar_tensor_tensor(x_raw[:, k, :], x_raw[:, k, :], g_col(k), pair(3),
                                           ALU.mult, ALU.mult).then_inc(h_scaled, 1)

        with dve.Fori(0, GB_BLOCKS // 4) as i:
            for j in range(4):
                split_lo(4 * i, j + 2)

        with dve.Fori(0, HEADS) as g:
            for s in range(4):
                split_lo(4 * g, SILU_0 + s + 2)
            dve.wait_ge(silu_out, TT * 16 * g + TT * 16)
            for t in range(TT):
                dve.wait_ge(sig_z_ready, TT * g + (t + 1))
                nc.vector.tensor_tensor(silu_z[:, t, :], psum[:, t, :], sig_z[:, t, :], ALU.mult)\
                    .then_inc(pair_read[t // 2], 1)

        dve.wait_ge(gate_b_out, 64 + 16 * KT)
        dve.wait_ge(silu_out, TT * 16 * (HEADS + 1))
        nc.vector.memset(u_pad[:, 0:CONV - 1], 0.0)
        with dve.Fori(0, KT) as c:
            def step(n):
                return CONV_STEPS * c + (CONV_STEPS + n)

            def conv_col(n):
                return cols[:, bass.ds(c + (1 + n) * KT, 1)]

            split_lo(4 * c, CONV_0 + 2)
            split_lo(4 * c, CONV_0 + 3)
            dve.wait_ge(pair_read[0], c + (READ_CONV + 1))
            dve.wait_ge(block_done, 4 * c + (RING + CONV_0 + 2))
            nc.vector.tensor_tensor(u_pad[:, CONV - 1:], pair(1), u_pad[:, CONV - 1:], ALU.mult)\
                .then_inc(pair_read[1], 1)
            dve.wait_ge(pair_read[1], c + (READ_CONV + 1))
            nc.vector.tensor_scalar(taps[:, :], u_pad[:, 0:T], conv_col(0), conv_col(CONV), ALU.mult, ALU.add)\
                .then_inc(conv_step, 1)
            for n in range(1, CONV):
                dve.wait_ge(conv_step, step(n))
                nc.vector.scalar_tensor_tensor(taps[:, :], u_pad[:, n:n + T], conv_col(n), taps[:, :],
                                               ALU.mult, ALU.add).then_inc(conv_step, 1)
            split_lo(4 * c, CONV_0 + 4)
            dve.wait_ge(sig_c_ready, c + 1)
            nc.vector.tensor_tensor(gate_zb[:, :], pair(2), gate_zb[:, :], ALU.mult)\
                .then_inc(pair_read[2], 1)
            split_lo(4 * c, CONV_0 + 5)
            dve.wait_ge(block_done, 4 * c + (RING + CONV_0 + 4))
            dve.wait_ge(pair_read[2], c + (READ_CONV + 1))
            nc.vector.tensor_tensor(gate_zb[:, :], pair(3), gate_zb[:, :], ALU.mult)\
                .then_inc(pair_read[3], 1)
            dve.wait_ge(pair_read[3], c + (READ_CONV + 1))
            dve.wait_ge(conv_step, step(3))
            nc.vector.tensor_tensor(taps[:, :], gate_zb[:, :], taps[:, :], ALU.mult).then_inc(conv_step, 1)
            dve.wait_ge(conv_step, step(4))
            nc.vector.tensor_scalar(y_hi[:, c, :], taps[:, :], 1.0, None, ALU.mult).then_inc(conv_step, 1)
            dve.wait_ge(conv_step, step(5))
            nc.vector.tensor_tensor(y_lo[:, c, :], taps[:, :], y_hi[:, c, :].bitcast(F32), ALU.subtract)\
                .then_inc(y_ready, 1)

        with dve.Fori(0, KT // 2) as i:
            for j in (1, 3):
                split_lo(4 * i, MIX_0 + j + 1)
                split_lo(4 * i, MIX_0 + j + 2)
                dve.wait_ge(block_done, 4 * i + (RING + MIX_0 + j + 1))
                dve.wait_ge(pair_read[j - 1], i + (READ_MIX + 1))
                dve.wait_ge(mixed_out, 32 * i + 32)
                nc.vector.tensor_tensor(mixed_a[:, j // 2, :], pair(j), sig_a[:, j // 2, :], ALU.mult)\
                    .then_inc(pair_read[j], 1)

        def rotate(h, j):
            lo, hi = ((q_lo, q_hi), (k_lo, k_hi))[j]
            cos, sin = rope_sb[:, 0, :], rope_sb[:, 1, :]
            one, two = pair(2 * j), pair(2 * j + 1)
            at = 2 * TURN_STEPS * h + TURN_STEPS * (1 + j)
            dve.wait_ge(block_done, HEAD_BLOCKS * h + (RING + HEAD_0 + 2 * j + 2))
            dve.wait_ge(turn_step, at)
            nc.vector.tensor_tensor(turn_1[:, :], one, cos, ALU.mult).then_inc(turn_step, 1)
            nc.vector.tensor_tensor(turn_2[:, :], two, sin, ALU.mult).then_inc(turn_step, 1)
            dve.wait_ge(turn_step, at + 2)
            nc.vector.tensor_tensor(turn_1[:, :], turn_1[:, :], turn_2[:, :], ALU.subtract).then_inc(turn_step, 1)
            dve.wait_ge(turn_step, at + 3)
            nc.vector.tensor_tensor(turn_2[:, :], one, sin, ALU.mult)\
                .then_inc(pair_read[2 * j], 1)
            dve.wait_ge(turn_hi_ready, 4 * h + (2 * j + 1))
            nc.vector.tensor_tensor(lo[:, 0, :], turn_1[:, :], hi[:, 0, :].bitcast(F32), ALU.subtract)\
                .then_inc(turn_step, 1)
            dve.wait_ge(turn_step, at + 4)
            nc.vector.tensor_tensor(turn_1[:, :], two, cos, ALU.mult)\
                .then_inc(pair_read[2 * j + 1], 1)
            for n in (2 * j, 2 * j + 1):
                dve.wait_ge(pair_read[n], head_read(n, h, 1))
            nc.vector.tensor_tensor(turn_2[:, :], turn_2[:, :], turn_1[:, :], ALU.add).then_inc(turn_step, 1)
            dve.wait_ge(turn_hi_ready, 4 * h + (2 * j + 2))
            nc.vector.tensor_tensor(lo[:, 1, :], turn_2[:, :], hi[:, 1, :].bitcast(F32), ALU.subtract)\
                .then_inc(turn_step, 1)

        def score(h, n):
            at = psum[:, n % 2, :]
            dve.wait_ge(bank_full[n % 2], full_head(0, h, 1 + n // 2))
            if n < TT - 1:
                nc.vector.tensor_scalar(at[:, P:P + QK], at[:, P:P + QK], key_decay, None, ALU.mult)
            nc.vector.tensor_tensor(at[:, 0:P], at[:, 0:P], decay, ALU.mult).then_inc(score_made, 1)
            parts = 2 if n < TT - 1 else 1
            dve.wait_ge(score_hi_ready, (2 * TT - 1) * h + (2 * n + parts))
            if n < TT - 1:
                nc.vector.tensor_tensor(key_lo[:, n % 2, :], at[:, P:P + QK], key_hi[:, n % 2, :].bitcast(F32),
                                        ALU.subtract)
            nc.vector.tensor_tensor(score_lo[:, n % 2, :], at[:, 0:P], score_hi[:, n % 2, :].bitcast(F32),
                                    ALU.subtract).then_inc(pair_read[0], 1)

        def new_state(h, n):
            for b in (2, 3):
                dve.wait_ge(bank_full[b], full_head(b, h, 1 + n))
            if n == 0:
                made = nc.vector.tensor_copy(state[:, :], pair(1))
            else:
                dve.wait_ge(state_ready, (TT - 1) * h + n)
                made = nc.vector.scalar_tensor_tensor(state[:, :], state[:, :], chunk_decay, pair(1), ALU.mult, ALU.add)
            made.then_inc(pair_read[1], 1)

        def gated_rows(h, n):
            dve.wait_ge(o_scale_ready, TT * h + (n + 1))
            dve.wait_ge(silu_back[n % 2], 64 * h + 16 * (n // 2 + 1))
            if n:
                dve.wait_ge(bank_full[6 + (n - 1) % 2], full_head(6 + (n - 1) % 2, h, 1 + (n - 1) // 2))
            nc.vector.scalar_tensor_tensor(o_rows[:, :], psum[:, 4 + n % 2, :], rms_scale[:, n % 2:n % 2 + 1],
                                           silu_in[:, n % 2, :], ALU.mult, ALU.mult)\
                .then_inc(pair_read[2], 1)

        with dve.Fori(0, HEADS) as h:
            for j in range(4):
                split_lo(HEAD_BLOCKS * h, HEAD_0 + j + 2)
                if j % 2:
                    dve.wait_ge(rope_in, 16 * h + 16)
                    rotate(h, j // 2)
            for s in range(4):
                split_lo(HEAD_BLOCKS * h, HEAD_0 + 4 + s + 2)
            for t in range(TT):
                dve.wait_ge(v_hi_ready, TT * h + (t + 1))
                nc.vector.tensor_tensor(v_lo[:, t, :], psum[:, t, :], v_hi[:, t, :].bitcast(F32), ALU.subtract)\
                    .then_inc(pair_read[t // 2], 1)
            dve.wait_ge(table_in, 16 * h + 16)
            score(h, 0)
            score(h, 1)
            new_state(h, 0)
            for n in range(TT):
                if n + 2 < TT:
                    score(h, n + 2)
                if n + 1 < TT - 1:
                    new_state(h, n + 1)
                gated_rows(h, n)

        def split_o_lo(i, e):
            dve.wait_ge(o_hi_ready, 4 * i + (e + 1))
            nc.vector.tensor_tensor(o_lo[:, e % RING, :], o_raw[:, e % RING, :], o_hi[:, e % RING, :].bitcast(F32),
                                    ALU.subtract).then_inc(o_ready, 1)

        split_o_lo(0, 0)
        split_o_lo(0, 1)
        for half in range(2):
            first, e0 = LAST_0 + half * HALF_BLOCKS, half * YB_BLOCKS
            for j in range(2):
                split_lo(0, first + j + 2)
                split_o_lo(0, e0 + j + 2)
            with dve.Fori(0, YB_BLOCKS // RING - 1) as i:
                for j in range(2, 2 + RING):
                    split_lo(4 * i, first + j + 2)
                    split_o_lo(i, e0 + j + 2)
            for j in range(YB_BLOCKS - 2, YB_BLOCKS):
                split_lo(0, first + j + 2)
            dve.wait_ge(gates_back, 32 * (half + 1))
            n0 = half * KT

            def gated(k):
                if k < BANKS - 1:
                    dve.wait_ge(bank_full[k], full_last(k, half, 0))
                else:
                    dve.wait_ge(block_done, RING + first + YB_BLOCKS)
                nc.vector.tensor_tensor(merged[:, k, :], psum[:, k, :], gate_b_in[:, k, :], ALU.mult)\
                    .then_inc(pair_read[k // 2], 1)

            def add_mixed(k):
                dve.wait_ge(pair_read[k // 2], last_read(k // 2, half, k % 2 + 1))
                nc.vector.tensor_tensor(merged[:, k, :], merged[:, k, :], mixed_in[:, k, :], ALU.add)\
                    .then_inc(merged_ready, 1)

            def merged_lo(k):
                dve.wait_ge(m_hi_ready, n0 + k + 1)
                nc.vector.tensor_tensor(m_lo[:, k, :], merged[:, k, :], m_hi[:, k, :].bitcast(F32), ALU.subtract)\
                    .then_inc(m_ready, 1)

            gated(0)
            gated(1)
            add_mixed(0)
            gated(2)
            merged_lo(0)
            for k in range(3, KT):
                gated(k)
            for k in range(1, KT):
                add_mixed(k)
                if first + YB_BLOCKS + k + 1 < STREAM:
                    split_lo(0, first + YB_BLOCKS + k + 1)
                merged_lo(k)
            if half == 0:
                split_lo(0, first + YB_BLOCKS + OUT_BLOCKS + 1)
                split_o_lo(0, YB_BLOCKS)
                split_o_lo(0, YB_BLOCKS + 1)
            dve.wait_ge(result_in, 16 * (half + 1))
            dve.wait_ge(final_in, 16)

            def add_x(t):
                dve.wait_ge(bank_full[2 * t], full_last(2 * t, half, 1))
                if t < OUT_TILES - 1:
                    dve.wait_ge(bank_full[2 * t + 1], full_last(2 * t + 1, half, 1))
                else:
                    dve.wait_ge(block_done, RING + first + HALF_BLOCKS)
                nc.vector.tensor_tensor(result[:, t, :], pair(t), result[:, t, :], ALU.add)\
                    .then_inc(pair_read[t], 1)

            def normed(t):
                dve.wait_ge(last_scale_ready, half * OUT_TILES + t + 1)
                nc.vector.scalar_tensor_tensor(result[:, t, :], result[:, t, :], rms_scale[:, t % 2:t % 2 + 1],
                                               final_sb[:, :], ALU.mult, ALU.mult).then_inc(result_ready, 1)

            add_x(0)
            for t in range(1, OUT_TILES):
                add_x(t)
                normed(t - 1)
            normed(OUT_TILES - 1)

    @block.tensor
    def _(pe):
        def product(dst, left, right, start, stop, l=slice(None), r=slice(None)):
            (l_hi, l_lo), (r_hi, r_lo) = left, right
            nc.tensor.matmul(dst, l_hi, r_hi, start=start, stop=False)
            nc.tensor.matmul(dst, l_hi, r_lo, start=False, stop=False)
            return nc.tensor.matmul(dst, l_lo, r_hi, start=False, stop=stop)

        def channel_block(b, n, j, read, hi, lo, arriving=False):
            pe.wait_ge(parts_ready, b + (n + 1))
            pe.wait_ge(pair_read[j], read)
            slot = n % RING
            for k in range(KT):
                if arriving:
                    pe.wait_ge(h_ready, k + 1)
                w = slice(k * P, (k + 1) * P)
                for part in range(2):
                    t = slice(part * BANK, (part + 1) * BANK)
                    last = product(psum[:, 2 * j + part, :], (w_hi[:, slot, w], w_lo[:, slot, w]),
                                   (hi[:, k, t], lo[:, k, t]), k == 0, k == KT - 1)
            last.then_inc(block_done, 1)

        def row_blocks(b, n, read):
            for s in range(4):
                pe.wait_ge(parts_ready, b + (n + s + 1))
                slot = (n + s) % RING
                for kk in range(2):
                    k = 2 * s + kk
                    for t in range(TT):
                        if k == 0 and t % 2 == 0:
                            pe.wait_ge(pair_read[t // 2], read(t // 2))
                        rows, c = slice(t * P, (t + 1) * P), slice(kk * V, (kk + 1) * V)
                        last = product(psum[:, t, :], (h_hi[:, k, rows], h_lo[:, k, rows]),
                                       (w_hi[:, slot, c], w_lo[:, slot, c]), k == 0, k == KT - 1)
                        if k == KT - 1 and t < BANKS - 1:
                            last.then_inc(bank_full[t], 1)
                last.then_inc(block_done, 1)

        pe.sem_inc(block_done, RING)

        pe.wait_ge(pool_consts, 2)
        for k in range(KT):
            pe.wait_ge(squares_ready, k + 1)
            for t in range(TT):
                last = nc.tensor.matmul(psum[:, 5, t:t + 1], squares[:, k, t * P:(t + 1) * P], ones[:, 0:1],
                                        start=(k == 0 and t == 0), stop=(k == KT - 1), skip_group_check=True)
        last.then_inc(sums_full, 1)
        for part in range(2):
            pe.wait_ge(diag_ready, (part + 1) * TT // 2)
            nc.tensor.matmul(psum[:, 6 + part, :], ones[:, :],
                             diagonal[:, part * TT // 2:(part + 1) * TT // 2, :].rearrange("p t n -> p (t n)"),
                             start=True, stop=True).then_inc(rms_full, 1)

        with pe.Fori(0, GB_BLOCKS // 4) as i:
            for j in range(4):
                channel_block(4 * i, j, j, i + READ_GB, h_hi, h_lo, arriving=j == 0)

        with pe.Fori(0, HEADS) as g:
            row_blocks(4 * g, SILU_0, lambda j: 2 * g + READ_SILU)

        with pe.Fori(0, KT) as c:
            for j in range(4):
                channel_block(4 * c, CONV_0 + j, j, c + READ_CONV, h_hi, h_lo)

        pe.wait_ge(y_ready, KT)
        with pe.Fori(0, KT // 2) as i:
            for j in range(4):
                hi, lo = (y_hi, y_lo) if j % 2 else (h_hi, h_lo)
                channel_block(4 * i, MIX_0 + j, j, i + READ_MIX, hi, lo)

        def chunk(n):
            return slice(n * P, (n + 1) * P)

        def scores(h, n):
            bank = n % 2
            pe.wait_ge(pair_read[0], head_read(0, h, 3 + max(n - 1, 0)))
            for d in range(DQ):
                last = product(psum[:, bank, 0:P], (k_hi[:, d, chunk(n)], k_lo[:, d, chunk(n)]),
                               (q_hi[:, d, chunk(n)], q_lo[:, d, chunk(n)]), d == 0, d == DQ - 1)
            if n < TT - 1:
                for d in range(DQ):
                    to = psum[:, bank, P + d * P:P + (d + 1) * P]
                    nc.tensor.matmul(to, k_hi[:, d, chunk(n)], ident_r[:, :], start=True, stop=False)
                    last = nc.tensor.matmul(to, k_lo[:, d, chunk(n)], ident_r[:, :], start=False, stop=True)
            last.then_inc(bank_full[bank], 1)

        def update(h, n):
            pe.wait_ge(pair_read[0], ret_read(0, h, n))
            pe.wait_ge(pair_read[1], head_read(1, h, 3 + n))
            for d in range(DQ):
                c = slice(d * P, (d + 1) * P)
                product(psum[:, 2 + d, :], (key_hi[:, n % 2, c], key_lo[:, n % 2, c]),
                        (v_hi[:, n, :], v_lo[:, n, :]), True, True).then_inc(bank_full[2 + d], 1)

        def rows(h, n):
            bank = 4 + n % 2
            pe.wait_ge(pair_read[2], head_read(2, h, 3 + max(n - 1, 0)))
            pe.wait_ge(pair_read[0], ret_read(0, h, n))
            last = product(psum[:, bank, :], (score_hi[:, n % 2, :], score_lo[:, n % 2, :]),
                           (v_hi[:, n, :], v_lo[:, n, :]), True, n == 0)
            if n:
                pe.wait_ge(state_ready, (TT - 1) * h + n)
                for d in range(DQ):
                    c = slice(d * V, (d + 1) * V)
                    last = product(psum[:, bank, :], (q_hi[:, d, chunk(n)], q_lo[:, d, chunk(n)]),
                                   (state_hi[:, (n - 1) % 2, c], state_lo[:, (n - 1) % 2, c]), False, d == DQ - 1)
            last.then_inc(bank_full[bank], 1)

        def transposed(h, n):
            bank = 6 + n % 2
            pe.wait_ge(pair_read[3], head_read(3, h, 3 + max(n - 1, 0)))
            pe.wait_ge(pair_read[2], ret_read(2, h, n))
            for e in range(ET):
                last = nc.tensor.transpose(psum[:, bank, e * P:(e + 1) * P], o_rows[:, e * P:(e + 1) * P], ident[:, :])
            last.then_inc(bank_full[bank], 1)

        pe.wait_ge(ident_ready, 1)
        with pe.Fori(0, HEADS) as h:
            for j in range(4):
                channel_block(HEAD_BLOCKS * h, HEAD_0 + j, j, head_read(j, h, 0), h_hi, h_lo)
            row_blocks(HEAD_BLOCKS * h, HEAD_0 + 4, lambda j: head_read(j, h, 1))
            pe.wait_ge(turn_step, 2 * TURN_STEPS * h + 3 * TURN_STEPS)
            scores(h, 0)
            scores(h, 1)
            for j in range(BANKS // 2):
                pe.wait_ge(pair_read[j], head_read(j, h, 3))
            update(h, 0)
            for n in range(TT):
                if n + 2 < TT:
                    scores(h, n + 2)
                rows(h, n)
                if n + 1 < TT - 1:
                    update(h, n + 1)
                if n:
                    transposed(h, n - 1)
            transposed(h, TT - 1)

        def o_block(i, half, e, start, stop):
            n = LAST_0 + half * HALF_BLOCKS + e
            pe.wait_ge(parts_ready, 4 * i + (n + 1))
            pe.wait_ge(o_ready, 4 * i + (half * YB_BLOCKS + e + 1))
            slot = e % RING
            for d in range(KT):
                if start and d % 2 == 0:
                    pe.wait_ge(pair_read[d // 2], last_read(d // 2, half, 0))
                w = slice(d * P, (d + 1) * P)
                last = product(psum[:, d, :], (w_hi[:, n % RING, w], w_lo[:, n % RING, w]),
                               (o_hi[:, slot, :], o_lo[:, slot, :]), start, stop)
                if stop and d < BANKS - 1:
                    last.then_inc(bank_full[d], 1)
            last.then_inc(block_done, 1)

        for half in range(2):
            for e in range(RING):
                o_block(0, half, e, e == 0, False)
            with pe.Fori(0, YB_BLOCKS // RING - 2) as i:
                for e in range(RING, 2 * RING):
                    o_block(i, half, e, False, False)
            for e in range(YB_BLOCKS - RING, YB_BLOCKS):
                o_block(0, half, e, False, e == YB_BLOCKS - 1)
            for k in range(OUT_BLOCKS):
                n = LAST_0 + half * HALF_BLOCKS + YB_BLOCKS + k
                pe.wait_ge(parts_ready, n + 1)
                pe.wait_ge(m_ready, half * KT + k + 1)
                for t in range(OUT_TILES):
                    for c in range(2):
                        bank = 2 * t + c
                        if k == 0 and c == 0:
                            pe.wait_ge(pair_read[t], last_read(t, half, 2))
                        left = (m_hi[:, k, chunk(t)], m_lo[:, k, chunk(t)])
                        w = slice(c * BANK, (c + 1) * BANK)
                        last = product(psum[:, bank, :], left, (w_hi[:, n % RING, w], w_lo[:, n % RING, w]),
                                       k == 0, k == OUT_BLOCKS - 1)
                        if k == OUT_BLOCKS - 1 and bank < BANKS - 1:
                            last.then_inc(bank_full[bank], 1)
                last.then_inc(block_done, 1)

    held.close()


def weight_stream(w_in, w_a, w_b, w_o):
    def channels(w, c0):
        return w[:, c0:c0 + P].reshape(KT, P, P).transpose(1, 0, 2).reshape(P, BLOCK)

    def columns(w, c0):
        return [w[2 * s * P:(2 * s + 2) * P, c0:c0 + V].reshape(2, P, V).transpose(1, 0, 2).reshape(P, BLOCK)
                for s in range(4)]

    b0, c0, x0, z0, q0, k0 = (n * D for n in range(6))
    v0, zb0, ga0, gb0 = 6 * D, 8 * D, 10 * D, 11 * D
    blocks = [channels(w_in, gb0 + d * P) for d in range(KT)]
    for h in range(HEADS):
        blocks += columns(w_in, zb0 + h * V)
    for c in range(KT):
        blocks += [channels(w_in, at + c * P) for at in (c0, x0, z0, b0)]
    for d in range(KT):
        blocks += [channels(w_in, ga0 + d * P), channels(w_a, d * P)]
    for h in range(HEADS):
        blocks += [channels(w_in, at + h * QK + d * P) for at in (q0, k0) for d in range(DQ)]
        blocks += columns(w_in, v0 + h * V)
    ends = [w_b[e * P:(e + 1) * P] for e in range(YB_BLOCKS)] + [w_o[k * P:(k + 1) * P] for k in range(OUT_BLOCKS)]
    return np.ascontiguousarray(np.stack(blocks + ends + ends))


def kernel(x, norm_g, w_in, conv_w, conv_b, w_a_out, w_b_out, w_o, final_g):
    import concourse.bacc as bacc
    from concourse.bass_utils import run_bass_kernel_spmd

    x2 = np.asarray(x)[0]
    rope, table, identity = constants()
    per_tile = [np.asarray(norm_g)[0], *np.asarray(conv_w)[0], np.asarray(conv_b)[0]]
    arrays = {
        "x_t": np.ascontiguousarray(x2.T.reshape(KT, P, T)),
        "x_rows": np.ascontiguousarray(x2.reshape(TT, P, D)),
        "columns": np.ascontiguousarray(np.concatenate([a.reshape(KT, P).T for a in per_tile], axis=1)),
        "weights": weight_stream(*(np.asarray(w)[0] for w in (w_in, w_a_out, w_b_out, w_o))),
        "final_g": np.ascontiguousarray(np.broadcast_to(np.asarray(final_g), (P, D))),
        "rope": rope,
        "head_table": table,
        "identity": identity,
    }
    nc = bacc.Bacc("TRN2", target_bir_lowering=False, num_devices=1)
    aps = [nc.dram_tensor(name, a.shape, mybir.dt.from_np(a.dtype), kind="ExternalInput").ap()
           for name, a in arrays.items()]
    out = nc.dram_tensor("out", (TT, P, D), F32, kind="ExternalOutput").ap()
    build(nc, *aps, out)
    r = run_bass_kernel_spmd(nc, [arrays], core_ids=[0])
    return r.results[0]["out"].reshape(1, T, D)
```

```python
from contextlib import ExitStack

import numpy as np
import concourse.bass as bass
from concourse import mybir

F32 = mybir.dt.float32
F32R = mybir.dt.float32r
BF16 = mybir.dt.bfloat16
ACT = mybir.ActivationFunctionType
ALU = mybir.AluOpType

P = 128
D = 1024
T = 1024
KT = D // P
TT = T // P
BANK = 512
BANKS = 8
BLOCK = 1024
HEADS = 4
QK = D // HEADS
DQ = QK // P
V = 2 * D // HEADS
ET = V // P
CHUNK = P
EPS = 1e-6
HALF = T // 2
CONV = 3
RING = 4
RAW = 2
X_RING = 4

GB_BLOCKS, CONV_BLOCKS, MIX_BLOCKS = KT, 4 * KT, 2 * KT
HEAD_BLOCKS, YB_BLOCKS, OUT_BLOCKS = 8 + ET, HEADS * ET, KT
SILU_0 = 8
CONV_0 = GB_BLOCKS
MIX_0 = CONV_0 + CONV_BLOCKS
HEAD_0 = MIX_0 + MIX_BLOCKS
LAST_0 = HEAD_0 + HEADS * HEAD_BLOCKS
HALF_BLOCKS = YB_BLOCKS + OUT_BLOCKS
STREAM = LAST_0 + 2 * HALF_BLOCKS

READ_GB = 1
READ_CONV = READ_GB + GB_BLOCKS // 4
READ_MIX = READ_CONV + KT
READ_HEAD = READ_MIX + MIX_BLOCKS // 4
HEAD_READS = [n + 3 for n in (TT, TT - 1, TT, TT)]
SILU_PARTS = 2 * ET


def head_read(j, h, n):
    return HEAD_READS[j] * h + (READ_HEAD + n)


def ret_read(j, h, n):
    return head_read(j, h, 3 + n + 1)


def last_read(j, half, n):
    return READ_HEAD + HEADS * HEAD_READS[j] + 3 * half + n


def full_head(bank, h, n):
    uses = [TT // 2, TT // 2, TT - 1, TT - 1, TT // 2, TT // 2, TT, SILU_PARTS // 2][bank]
    return uses * h + n if bank == 7 else (1 + uses) * h + (n + 1)


def full_last(bank, half, n):
    return full_head(bank, HEADS, 0) + 2 * half + n


def constants():
    freq = (10000.0 ** (-(np.arange(0, QK, 2, dtype=np.float32) / np.float32(QK)).astype(np.float64)))
    freq = freq.astype(np.float32)
    angle = (np.arange(T, dtype=np.float32)[None, :] * freq[:, None]).astype(np.float64)
    rope = np.stack([np.cos(angle), np.sin(angle)]).astype(np.float32)
    table = np.zeros((HEADS, P, P + 4), np.float64)
    j = np.arange(P, dtype=np.float64)
    for h in range(HEADS):
        gamma = 1.0 - 2.0 ** (-5.0 - h)
        xi = gamma ** (j + 1)
        table[h, :, :P] = (j[None, :] >= j[:, None]) * (gamma ** -(j + 1))[:, None] * QK ** -0.5
        table[h, :, P] = gamma ** (CHUNK - 1 - j) * QK ** -0.5
        table[h, :, P + 1] = xi / np.sqrt(V)
        table[h, :, P + 2] = xi
        table[h, :, P + 3] = gamma ** CHUNK
    return rope, table.astype(np.float32), np.eye(P, dtype=np.float32)


def build(nc, x_t, x_rows, columns, weights, final_g, rope, head_table, identity, out):
    gate_b_d = nc.dram_tensor("gate_b_scratch", (KT, P, T), F32, kind="Internal").ap()
    mixed_a_d = nc.dram_tensor("mixed_a_scratch", (KT, P, T), F32, kind="Internal").ap()
    silu_d = nc.dram_tensor("silu_scratch", (HEADS * ET, P, T), F32, kind="Internal").ap()
    o_d = nc.dram_tensor("o_scratch", (2, HEADS * ET, P, HALF), F32, kind="Internal").ap()

    held = ExitStack()

    def sb(stack, name, shape, dt):
        return stack.enter_context(nc.sbuf_tensor(name, shape, dt))

    def sem(name):
        return held.enter_context(nc.semaphore(name))

    w_hi = sb(held, "w_hi", [P, RING, BLOCK], F32R)
    w_lo = sb(held, "w_lo", [P, RING, BLOCK], F32R)
    w_raw = sb(held, "w_raw", [P, RAW, BLOCK], F32)
    ident = sb(held, "ident", [P, P], F32)
    ident_r = sb(held, "ident_r", [P, P], F32R)
    NCOL = KT * (2 + CONV)
    cols = sb(held, "cols", [P, NCOL], F32)
    small = sb(held, "small", [P, 4 * TT + 1], F32)
    rms_var, rms_scale, minus_half = (small[:, n * TT:(n + 1) * TT] for n in range(3))
    square_sum = small[:, 3 * TT:4 * TT]
    eps = small[:, 4 * TT:4 * TT + 1]
    psum = held.enter_context(nc.psum_tensor("psum", [P, BANKS, BANK], F32))

    def g_col(k):
        return cols[:, k:k + 1]

    with ExitStack() as s:
        rows_raw = sb(s, "rows_raw", [P, TT, D], F32)
        diagonal = sb(s, "diagonal", [P, TT, P], F32)
        ones = sb(s, "ones", [P, P], F32)
    with ExitStack() as upper:
        h_hi = sb(upper, "h_hi", [P, KT, T], F32R)
        h_lo = sb(upper, "h_lo", [P, KT, T], F32R)
        with ExitStack() as s:
            xg_hi = sb(s, "xg_hi", [P, KT, T], F32R)
            xg_lo = sb(s, "xg_lo", [P, KT, T], F32R)
            x_raw = sb(s, "x_raw", [P, X_RING, T], F32)
            gate_b = sb(s, "gate_b", [P, 4, T], F32)
            factors = sb(s, "factors", [P, T], F32)
        with ExitStack() as s:
            y_hi = sb(s, "y_hi", [P, KT, T], F32R)
            y_lo = sb(s, "y_lo", [P, KT, T], F32R)
            with ExitStack() as s2:
                u_pad = sb(s2, "u_pad", [P, T + CONV - 1], F32)
                taps = sb(s2, "taps", [P, T], F32)
                gate_zb = sb(s2, "gate_zb", [P, T], F32)
            with ExitStack() as s2:
                sig_a = sb(s2, "sig_a", [P, 2, T], F32)
                mixed_a = sb(s2, "mixed_a", [P, 2, T], F32)
        with ExitStack() as s:
            k_hi = sb(s, "k_hi", [P, DQ, T], F32R)
            k_lo = sb(s, "k_lo", [P, DQ, T], F32R)
            v_parts = sb(s, "v_parts", [P, TT, 2, V], F32R)
            q_hi = sb(s, "q_hi", [P, DQ, T], F32R)
            q_lo = sb(s, "q_lo", [P, DQ, T], F32R)
            state_hi = sb(s, "state_hi", [P, 2, DQ * V], F32R)
            state_lo = sb(s, "state_lo", [P, 2, DQ * V], F32R)
            score_hi = sb(s, "score_hi", [P, 2, P], F32R)
            score_lo = sb(s, "score_lo", [P, 2, P], F32R)
            key_hi = sb(s, "key_hi", [P, 2, QK], F32R)
            key_lo = sb(s, "key_lo", [P, 2, QK], F32R)
            with ExitStack() as s2:
                rope_sb = sb(s2, "rope_sb", [P, 2, T], F32)
                turn_1 = sb(s2, "turn_1", [P, T], F32)
                turn_2 = sb(s2, "turn_2", [P, T], F32)
            with ExitStack() as s2:
                state = sb(s2, "state", [P, DQ * V], F32)
                o_t = sb(s2, "o_t", [P, 2, ET, P], F32)
                o_rows = sb(s2, "o_rows", [P, V], F32)
                table = sb(s2, "table", [P, P + 4], F32)
                unused = sb(s2, "unused", [P, V], BF16)
                silu_z = sb(s2, "silu_z", [P, T], F32)
    with ExitStack() as last:
        m_hi = sb(last, "m_hi", [P, KT, HALF], F32R)
        m_lo = sb(last, "m_lo", [P, KT, HALF], F32R)
        merged = sb(last, "merged", [P, KT, HALF], F32)
        result = sb(last, "result", [P, 4, D], F32)
        o_hi = sb(last, "o_hi", [P, RING, HALF], F32R)
        o_lo = sb(last, "o_lo", [P, RING, HALF], F32R)
        o_raw = sb(last, "o_raw", [P, RING, HALF], F32)
        silu_raw = sb(last, "silu_raw", [P, RING, HALF], F32)
        gate_b_in = sb(last, "gate_b_in", [P, KT, HALF], F32)
        mixed_in = sb(last, "mixed_in", [P, KT, HALF], F32)
        final_sb = sb(last, "final_sb", [P, D], F32)
        unused_last = sb(last, "unused_last", [P, D], BF16)

    v_hi, v_lo = v_parts[:, :, 0, :], v_parts[:, :, 1, :]
    decay, key_decay, xi_mean, xi, chunk_decay = (
        table[:, 0:P], table[:, P:P + 1], table[:, P + 1:P + 2], table[:, P + 2:P + 3], table[:, P + 3:P + 4])

    raw_in = [sem(f"raw_in{n}") for n in range(RAW)]
    hi_ready = sem("hi_ready")
    parts_ready = sem("parts_ready")
    block_done = sem("block_done")
    bank_full = [sem(f"bank_full{b}") for b in range(BANKS)]
    pair_read = [sem(f"pair_read{j}") for j in range(BANKS // 2)]
    consts_in = sem("consts_in")
    ident_in = sem("ident_in")
    x_in = [sem(f"x_in{n}") for n in range(X_RING)]
    rows_in = [sem(f"rows_in{t}") for t in range(TT)]
    pool_consts = sem("pool_consts")
    ident_ready = sem("ident_ready")
    xg_hi_ready = sem("xg_hi_ready")
    xg_ready = sem("xg_ready")
    squares_ready = sem("squares_ready")
    var_ready = sem("var_ready")
    rms_ready = sem("rms_ready")
    diag_ready = sem("diag_ready")
    factors_full = sem("factors_full")
    h_scaled = sem("h_scaled")
    h_hi_ready = sem("h_hi_ready")
    h_ready = [sem(f"h_ready{n}") for n in range(2)]
    gate_b_ready = sem("gate_b_ready")
    gate_b_out = sem("gate_b_out")
    sig_c_ready = sem("sig_c_ready")
    conv_step = sem("conv_step")
    y_ready = sem("y_ready")
    mixed_out = sem("mixed_out")
    rope_in = sem("rope_in")
    turn_step = sem("turn_step")
    turn_hi_ready = sem("turn_hi_ready")
    v_hi_ready = sem("v_hi_ready")
    table_in = sem("table_in")
    sig_z_ready = sem("sig_z_ready")
    silu_read = sem("silu_read")
    silu_out = sem("silu_out")
    score_made = sem("score_made")
    score_hi_ready = sem("score_hi_ready")
    state_hi_ready = sem("state_hi_ready")
    state_ready = sem("state_ready")
    o_square_ready = sem("o_square_ready")
    o_var_ready = sem("o_var_ready")
    o_scale_ready = sem("o_scale_ready")
    o_out = [sem(f"o_out{n}") for n in range(2)]
    o_back = [sem(f"o_back{n}") for n in range(RING)]
    first_back = [sem(f"first_back{n}") for n in range(RING)]
    silu_back = [sem(f"silu_back{n}") for n in range(RING)]
    o_gated = sem("o_gated")
    o_hi_ready = sem("o_hi_ready")
    o_ready = sem("o_ready")
    gates_back = sem("gates_back")
    merged_ready = sem("merged_ready")
    m_hi_ready = sem("m_hi_ready")
    m_ready = sem("m_ready")
    result_in = sem("result_in")
    final_in = sem("final_in")
    last_square_ready = sem("last_square_ready")
    last_var_ready = sem("last_var_ready")
    last_scale_ready = sem("last_scale_ready")
    result_ready = sem("result_ready")
    first_out = sem("first_out")
    result_out = sem("result_out")

    CONV_STEPS, TURN_STEPS = 5, 6
    OUT_TILES = HALF // P

    def pair(j):
        return psum[:, 2 * j:2 * j + 2, :].rearrange("p b n -> p (b n)")

    block = held.enter_context(nc.Block())

    @block.sync
    def _(sp):
        def load_block(b, offset):
            n = offset + RAW + 2
            sp.wait_ge(parts_ready, b + (n - RAW + 1))
            sp.dma_start(w_raw[:, n % RAW, :], weights[b + n]).then_inc(raw_in[n % RAW], 16)

        sp.sem_inc(silu_out, 16)
        sp.sem_inc(mixed_out, 2 * 16)
        for n in range(2):
            sp.sem_inc(o_out[n], 16)

        def load_x(n):
            sp.dma_start(x_raw[:, n % X_RING, :], x_t[n % KT]).then_inc(x_in[n % X_RING], 16)

        def load_rows(t):
            sp.dma_start(rows_raw[:, t, :], x_rows[t]).then_inc(rows_in[t], 16)

        load_x(0)
        sp.dma_start(cols[:, :], columns).then_inc(consts_in, 16)
        sp.dma_start(w_raw[:, 0, :], weights[0]).then_inc(raw_in[0], 16)
        for k in range(1, X_RING):
            load_x(k)
        for k in range(X_RING, KT):
            sp.wait_ge(xg_ready, k - X_RING + 1)
            load_x(k)
        sp.dma_start(w_raw[:, 1, :], weights[1]).then_inc(raw_in[1], 16)
        sp.dma_start(ident[:, :], identity).then_inc(ident_in, 16)
        for t in range(TT // 2):
            load_rows(t)
        load_block(0, -2)
        for t in range(TT // 2, TT):
            load_rows(t)
        load_block(0, -1)
        for k in range(X_RING):
            sp.wait_ge(xg_ready, k + X_RING + 1)
            load_x(KT + k)
        load_block(0, 0)

        for k in range(X_RING, KT):
            sp.wait_ge(h_ready[k % 2], (k - X_RING) // 2 + 1)
            load_x(KT + k)
        for b in range(GB_BLOCKS):
            if b:
                load_block(0, b)
            if b < 4:
                sp.wait_ge(gate_b_ready, b + 1)
            else:
                sp.wait_ge(pair_read[b - 4], READ_GB + 2)
            sp.dma_start(gate_b_d[b], gate_b[:, b % 4, :]).then_inc(gate_b_out, 16)

        with sp.Fori(0, KT) as c:
            for j in range(4):
                load_block(4 * c, CONV_0 + j)

        with sp.Fori(0, KT // 2) as i:
            for j in range(4):
                load_block(4 * i, MIX_0 + j)
                if j % 2:
                    sp.wait_ge(pair_read[j], i + (READ_MIX + 1))
                    sp.dma_start(mixed_a_d[2 * i + j // 2], mixed_a[:, j // 2, :]).then_inc(mixed_out, 16)

        with sp.Fori(0, HEADS) as h:
            for n in range(2):
                sp.wait_ge(o_out[n], 64 * h + 16)
            sp.wait_ge(silu_out, 64 * h + 16)
            sp.wait_ge(mixed_out, (2 + KT) * 16)
            sp.dma_start(rope_sb[:, :, :], rope.rearrange("c p t -> p c t")).then_inc(rope_in, 16)

            def store_silu(m):
                sp.wait_ge(silu_read, SILU_PARTS * h + (SILU_PARTS + 2 * m + 2))
                sp.dma_start(silu_d[ET * h + m], silu_z[:, :]).then_inc(silu_out, 16)

            def store_o(n):
                sp.wait_ge(pair_read[3], ret_read(3, h, n))
                at = (n % 4) * P
                sp.dma_start(o_d[n // 4].rearrange("(h e) p c -> h p e c", e=ET)[h, :, :, at:at + P],
                             o_t[:, n % 2, :, :]).then_inc(o_out[n % 2], 16)

            for j in range(SILU_0):
                load_block(HEAD_BLOCKS * h, HEAD_0 + j)
                if j == 5:
                    sp.wait_ge(turn_step, 2 * TURN_STEPS * h + 3 * TURN_STEPS)
                    sp.wait_ge(turn_hi_ready, 4 * h + 4)
                    sp.dma_start(table[:, :], head_table[h]).then_inc(table_in, 16)
            for n in range(TT):
                if n % 2 == 0:
                    load_block(HEAD_BLOCKS * h, HEAD_0 + SILU_0 + n // 2)
                    if n < TT - 2:
                        store_silu(n // 2)
                if n:
                    store_o(n - 1)
            store_silu(ET - 1)
            store_o(TT - 1)

        def load_o(half, e):
            sp.dma_start(o_raw[:, e % RING, :], o_d[half, e]).then_inc(o_back[e % RING], 16)
            sp.dma_start(silu_raw[:, e % RING, :], silu_d[e, :, half * HALF:(half + 1) * HALF])\
                .then_inc(silu_back[e % RING], 16)

        for n in range(2):
            sp.wait_ge(o_out[n], 64 * HEADS + 16)
        sp.wait_ge(silu_out, 64 * HEADS + 16)
        for half in range(2):
            first = LAST_0 + half * HALF_BLOCKS
            at = half * HALF
            if half:
                sp.wait_ge(merged_ready, half * KT)
            sp.dma_start(gate_b_in[:, :, :], gate_b_d[:, :, at:at + HALF].rearrange("k p t -> p k t"))\
                .then_inc(gates_back, 16)
            sp.dma_start(mixed_in[:, :, :], mixed_a_d[:, :, at:at + HALF].rearrange("k p t -> p k t"))\
                .then_inc(gates_back, 16)
            if half == 0:
                sp.dma_start(final_sb[:, :], final_g).then_inc(final_in, 16)
            with sp.Fori(0, YB_BLOCKS // RING - 1) as i:
                for j in range(RING):
                    load_block(4 * i, first + j)
                    sp.wait_ge(o_ready, 4 * i + (half * YB_BLOCKS + j + 1))
                    sp.dma_start(o_raw[:, j, :], o_d[half, 4 * i + (j + RING)]).then_inc(o_back[j], 16)
                    sp.dma_start(silu_raw[:, j, :], silu_d[4 * i + (j + RING), :, at:at + HALF])\
                        .then_inc(silu_back[j], 16)
            for j in range(RING):
                load_block(0, first + YB_BLOCKS - RING + j)
            if half:
                sp.wait_ge(first_out, 16 * OUT_TILES)
            sp.dma_start(result[:, :, :], x_rows[half * OUT_TILES:(half + 1) * OUT_TILES].rearrange("t p n -> p t n"))\
                .then_inc(result_in, 16)
            for k in range(OUT_BLOCKS):
                if first + YB_BLOCKS + k + RAW + 2 < STREAM:
                    load_block(0, first + YB_BLOCKS + k)
                if half == 0 and k < RING:
                    sp.wait_ge(o_ready, YB_BLOCKS - RING + k + 1)
                    load_o(1, k)
        for t in range(OUT_TILES):
            sp.wait_ge(result_ready, OUT_TILES + t + 1)
            sp.dma_start(out[OUT_TILES + t], result[:, t, :]).then_inc(result_out, 16)
        sp.wait_ge(result_out, OUT_TILES * 16)

    @block.gpsimd
    def _(pool):
        pool.memset(ones[:, :], 1.0).then_inc(pool_consts, 1)
        pool.memset(minus_half, -0.5).then_inc(pool_consts, 1)
        pool.memset(eps, EPS).then_inc(pool_consts, 1)
        pool.wait_ge(pool_consts, 3)
        pool.wait_ge(var_ready, 1)
        nc.gpsimd.tensor_tensor(rms_scale, rms_var, minus_half, ALU.pow).then_inc(rms_ready, 1)
        for k in range(1, KT, 2):
            pool.wait_ge(h_hi_ready, k + 1)
            nc.gpsimd.tensor_tensor(h_lo[:, k, :], x_raw[:, k % X_RING, :], h_hi[:, k, :].bitcast(F32), ALU.subtract)\
                .then_inc(h_ready[1], 1)

        def o_factor(h, n):
            v = rms_var[:, n % 2:n % 2 + 1]
            r = rms_scale[:, n % 2:n % 2 + 1]
            pool.wait_ge(o_square_ready, TT * h + (n + 1))
            nc.gpsimd.tensor_tensor(v, square_sum[:, n % 2:n % 2 + 1], eps, ALU.add)\
                .then_inc(o_var_ready, 1)
            pool.wait_ge(o_var_ready, 2 * TT * h + (2 * n + 1))
            nc.gpsimd.tensor_tensor(r, v, minus_half[:, 0:1], ALU.pow).then_inc(o_var_ready, 1)
            pool.wait_ge(o_var_ready, 2 * TT * h + (2 * n + 2))
            nc.gpsimd.tensor_tensor(r, r, xi, ALU.mult).then_inc(o_scale_ready, 1)

        with pool.Fori(0, HEADS) as h:
            pool.wait_ge(table_in, 16 * h + 16)
            for n in range(TT):
                o_factor(h, n)

        pool.wait_ge(pair_read[2], ret_read(2, HEADS - 1, TT // 2 - 1))
        for n in range(2):
            pool.wait_ge(o_out[n], 64 + 16)
        pool.wait_ge(silu_out, 64 + 16)
        for e in range(RING):
            pool.dma_start(o_raw[:, e, :], o_d[0, e]).then_inc(first_back[e], 16)
            pool.dma_start(silu_raw[:, e, :], silu_d[e, :, 0:HALF]).then_inc(first_back[e], 16)

        for t in range(2 * OUT_TILES):
            if t == OUT_TILES:
                pool.wait_ge(result_ready, t)
                pool.dma_start(out[t - 1], result[:, t - 1, :]).then_inc(first_out, 16)
            v, r = rms_var[:, t % 2:t % 2 + 1], rms_scale[:, t % 2:t % 2 + 1]
            pool.wait_ge(last_square_ready, t + 1)
            nc.gpsimd.tensor_scalar(v, square_sum[:, t % 2:t % 2 + 1], 1.0 / D, EPS, ALU.mult, ALU.add)\
                .then_inc(last_var_ready, 1)
            pool.wait_ge(last_var_ready, t + 1)
            nc.gpsimd.tensor_tensor(r, v, minus_half[:, 0:1], ALU.pow).then_inc(last_scale_ready, 1)
            if 1 <= t < OUT_TILES:
                pool.wait_ge(result_ready, t)
                pool.dma_start(out[t - 1], result[:, t - 1, :]).then_inc(first_out, 16)

    @block.scalar
    def _(act):
        def split_hi(b, offset):
            n = offset
            act.wait_ge(raw_in[n % RAW], 8 * b + 16 * (n // RAW + 1))
            act.wait_ge(block_done, b + (n + 1))
            nc.scalar.activation(w_hi[:, n % RING, :], w_raw[:, n % RAW, :], ACT.Copy).then_inc(hi_ready, 1)

        act.wait_ge(consts_in, 16)
        for k in range(KT):
            act.wait_ge(x_in[k % X_RING], 16 * (k // X_RING + 1))
            nc.scalar.activation(xg_hi[:, k, :], x_raw[:, k % X_RING, :], ACT.Copy, scale=g_col(k))\
                .then_inc(xg_hi_ready, 1)
            if k == 0:
                split_hi(0, 0)
        split_hi(0, 1)
        act.wait_ge(ident_in, 16)
        nc.scalar.activation(ident_r[:, :], ident[:, :], ACT.Copy).then_inc(ident_ready, 1)
        for t in range(TT):
            act.wait_ge(rows_in[t], 16)
            nc.scalar.activation(rows_raw[:, t, :], rows_raw[:, t, :], ACT.Square,
                                 accum_out=square_sum[:, t:t + 1]).then_inc(squares_ready, 1)
            if t == TT // 2:
                split_hi(0, 2)
        split_hi(0, 3)

        def scaled_gate(j):
            act.wait_ge(pair_read[j], READ_GB + 1)
            nc.scalar.activation(gate_b[:, j, :], gate_b[:, j, :], ACT.Sigmoid).then_inc(gate_b_ready, 1)

        for k in range(KT):
            if k == 2:
                split_hi(0, 4)
                scaled_gate(0)
            act.wait_ge(h_scaled, k + 1)
            nc.scalar.activation(h_hi[:, k, :], x_raw[:, k % X_RING, :], ACT.Copy).then_inc(h_hi_ready, 1)
        split_hi(0, 5)
        for j in range(1, 4):
            scaled_gate(j)
        for j in range(4):
            split_hi(0, 4 + j + 2)
            act.wait_ge(block_done, RING + 4 + j + 1)
            act.wait_ge(gate_b_out, 64)
            nc.scalar.activation(gate_b[:, j, :], pair(j), ACT.Sigmoid).then_inc(pair_read[j], 1)

        act.wait_ge(gate_b_out, 16 * KT)
        with act.Fori(0, KT) as c:
            split_hi(4 * c, CONV_0 + 2)
            act.wait_ge(block_done, 4 * c + (RING + CONV_0 + 1))
            act.wait_ge(conv_step, CONV_STEPS * c + 3)
            nc.scalar.activation(u_pad[:, CONV - 1:], pair(0), ACT.Copy).then_inc(pair_read[0], 1)
            split_hi(4 * c, CONV_0 + 3)
            split_hi(4 * c, CONV_0 + 4)
            act.wait_ge(block_done, 4 * c + (RING + CONV_0 + 3))
            act.wait_ge(conv_step, CONV_STEPS * c + 4)
            nc.scalar.activation(gate_zb[:, :], pair(2), ACT.Sigmoid).then_inc(sig_c_ready, 1)
            split_hi(4 * c, CONV_0 + 5)

        act.wait_ge(y_ready, KT)
        with act.Fori(0, KT // 2) as i:
            for j in (0, 2):
                split_hi(4 * i, MIX_0 + j + 2)
                act.wait_ge(block_done, 4 * i + (RING + MIX_0 + j + 1))
                act.wait_ge(pair_read[j + 1], i + READ_MIX)
                nc.scalar.activation(sig_a[:, j // 2, :], pair(j), ACT.Sigmoid).then_inc(pair_read[j], 1)
                split_hi(4 * i, MIX_0 + j + 3)

        def score_parts(h, n):
            act.wait_ge(score_made, TT * h + (n + 1))
            if n >= 2:
                act.wait_ge(bank_full[4 + n % 2], full_head(4, h, 1 + (n - 2) // 2))
            nc.scalar.activation(score_hi[:, n % 2, :], psum[:, n % 2, 0:P], ACT.Copy).then_inc(score_hi_ready, 1)
            if n < TT - 1:
                nc.scalar.activation(key_hi[:, n % 2, :], psum[:, n % 2, P:P + QK], ACT.Copy)\
                    .then_inc(score_hi_ready, 1)

        def state_parts(h, n):
            act.wait_ge(pair_read[1], ret_read(1, h, n))
            if n >= 2:
                act.wait_ge(bank_full[4 + (n - 1) % 2], full_head(4, h, 1 + (n - 1) // 2))
            nc.scalar.activation(state_hi[:, n % 2, :], state[:, :], ACT.Copy).then_inc(state_hi_ready, 1)

        def o_back_copy(h, n):
            act.wait_ge(bank_full[6], full_head(6, h, 1 + n))
            act.wait_ge(o_out[n % 2], 64 * h + 16 * (n // 2 + 1))
            nc.scalar.activation(o_t[:, n % 2, :, :].rearrange("p e c -> p (e c)"), psum[:, 6, :], ACT.Copy)\
                .then_inc(pair_read[3], 1)

        with act.Fori(0, HEADS) as h:
            for j in range(4):
                split_hi(HEAD_BLOCKS * h, HEAD_0 + j + 2)
                if j % 2:
                    for d, part in enumerate((turn_1, turn_2)):
                        dst = (q_hi, k_hi)[j // 2]
                        act.wait_ge(turn_step, 2 * TURN_STEPS * h + (TURN_STEPS * (1 + j // 2) + (3, 5)[d]))
                        nc.scalar.activation(dst[:, d, :], part[:, :], ACT.Copy).then_inc(turn_hi_ready, 1)
            for s in range(4):
                split_hi(HEAD_BLOCKS * h, HEAD_0 + 4 + s + 2)
            for t in range(TT):
                if t < BANKS - 1:
                    act.wait_ge(bank_full[t], full_head(t, h, 0))
                else:
                    act.wait_ge(block_done, HEAD_BLOCKS * h + (RING + HEAD_0 + SILU_0))
                nc.scalar.activation(v_hi[:, t, :], psum[:, t, :], ACT.Copy).then_inc(v_hi_ready, 1)
            score_parts(h, 0)
            score_parts(h, 1)
            act.wait_ge(table_in, 16 * h + 16)

            def silu_sigmoid(m):
                at = (m % 2) * HALF
                if m % 2 == 0:
                    split_hi(HEAD_BLOCKS * h, HEAD_0 + SILU_0 + m // 2 + 2)
                    act.wait_ge(bank_full[7], full_head(7, h, m // 2 + 1))
                    act.wait_ge(silu_out, 64 * h + (16 * (m // 2) + 16))
                else:
                    act.wait_ge(block_done, HEAD_BLOCKS * h + (RING + HEAD_0 + SILU_0 + m // 2 + 1))
                nc.scalar.activation(silu_z[:, at:at + HALF], psum[:, 7, :], ACT.Sigmoid).then_inc(sig_z_ready, 1)

            def o_squares(n):
                act.wait_ge(bank_full[4 + n % 2], full_head(4, h, 1 + n // 2))
                if n:
                    act.wait_ge(o_square_ready, TT * h + n)
                nc.scalar.activation(unused[:, :], psum[:, 4 + n % 2, :], ACT.Square, scale=xi_mean,
                                     accum_out=square_sum[:, n % 2:n % 2 + 1]).then_inc(o_square_ready, 1)

            def o_scaled(n):
                act.wait_ge(o_scale_ready, TT * h + (n + 1))
                nc.scalar.activation(o_rows[:, :], psum[:, 4 + n % 2, :], ACT.Copy, scale=rms_scale[:, n % 2:n % 2 + 1])\
                    .then_inc(pair_read[2], 1)

            silu_sigmoid(0)
            state_parts(h, 0)
            for n in range(TT):
                if n + 2 < TT:
                    score_parts(h, n + 2)
                o_squares(n)
                if n + 1 < TT - 1:
                    state_parts(h, n + 1)
                    silu_sigmoid(n + 1)
                if n:
                    o_back_copy(h, n - 1)
                o_scaled(n)
            silu_sigmoid(SILU_PARTS - 1)
            o_back_copy(h, TT - 1)

        def split_o_hi(i, e):
            act.wait_ge(o_gated, 4 * i + (e + 1))
            if e >= RING:
                half, tile = divmod(e - RING, YB_BLOCKS)
                act.wait_ge(block_done, 4 * i + (RING + LAST_0 + half * HALF_BLOCKS + tile + 1))
            nc.scalar.activation(o_hi[:, e % RING, :], o_raw[:, e % RING, :], ACT.Copy).then_inc(o_hi_ready, 1)

        split_o_hi(0, 0)
        split_o_hi(0, 1)
        for half in range(2):
            first, e0 = LAST_0 + half * HALF_BLOCKS, half * YB_BLOCKS
            for j in range(2):
                split_hi(0, first + j + 2)
                split_o_hi(0, e0 + j + 2)
            with act.Fori(0, YB_BLOCKS // RING - 1) as i:
                for j in range(2, 2 + RING):
                    split_hi(4 * i, first + j + 2)
                    split_o_hi(i, e0 + j + 2)
            for j in range(YB_BLOCKS - 2, YB_BLOCKS):
                split_hi(0, first + j + 2)
            for k in range(KT):
                act.wait_ge(merged_ready, half * KT + k + 1)
                if half and k == 0:
                    act.wait_ge(block_done, RING + LAST_0 + HALF_BLOCKS)
                nc.scalar.activation(m_hi[:, k, :], merged[:, k, :], ACT.Copy).then_inc(m_hi_ready, 1)
                if first + YB_BLOCKS + k + 2 < STREAM:
                    split_hi(0, first + YB_BLOCKS + k + 2)
            if half == 0:
                split_o_hi(0, YB_BLOCKS)
                split_o_hi(0, YB_BLOCKS + 1)
            for t in range(OUT_TILES):
                act.wait_ge(pair_read[t], last_read(t, half, 3))
                if half or t:
                    act.wait_ge(last_square_ready, half * OUT_TILES + t)
                nc.scalar.activation(unused_last[:, :], result[:, t, :], ACT.Square,
                                     accum_out=square_sum[:, t % 2:t % 2 + 1]).then_inc(last_square_ready, 1)

    @block.vector
    def _(dve):
        def split_lo(b, offset):
            n = offset
            dve.wait_ge(hi_ready, b + (n + 1))
            nc.vector.tensor_tensor(w_lo[:, n % RING, :], w_raw[:, n % RAW, :], w_hi[:, n % RING, :].bitcast(F32),
                                    ALU.subtract).then_inc(parts_ready, 1)

        for j in range(3):
            dve.sem_inc(pair_read[j], 1)
        dve.sem_inc(conv_step, CONV_STEPS)
        dve.sem_inc(turn_step, TURN_STEPS)
        dve.sem_inc(silu_read, SILU_PARTS)

        dve.wait_ge(consts_in, 16)
        for k in range(KT):
            dve.wait_ge(xg_hi_ready, k + 1)
            nc.vector.scalar_tensor_tensor(xg_lo[:, k, :], x_raw[:, k % X_RING, :], g_col(k),
                                           xg_hi[:, k, :].bitcast(F32), ALU.mult, ALU.subtract)\
                .then_inc(xg_ready, 1)
            if k == 0:
                split_lo(0, 0)
        split_lo(0, 1)
        split_lo(0, 2)
        dve.wait_ge(squares_ready, TT)
        nc.vector.tensor_scalar(rms_var, square_sum, 1.0 / D, EPS, ALU.mult, ALU.add).then_inc(var_ready, 1)
        split_lo(0, 3)
        dve.wait_ge(rms_ready, 1)
        dve.wait_ge(ident_in, 16)
        for t in range(TT):
            nc.vector.tensor_scalar(diagonal[:, t, :], ident[:, :], rms_scale[:, t:t + 1], None, ALU.mult)\
                .then_inc(diag_ready, 1)
        dve.wait_ge(factors_full, 2)
        nc.vector.tensor_copy(factors[:, :], pair(3)).then_inc(pair_read[3], 1)

        def scaled_gate(j):
            dve.wait_ge(block_done, RING + j + 1)
            nc.vector.tensor_tensor(gate_b[:, j, :], pair(j), factors[:, :], ALU.mult).then_inc(pair_read[j], 1)

        def h_low(k):
            dve.wait_ge(h_hi_ready, k + 1)
            nc.vector.tensor_tensor(h_lo[:, k, :], x_raw[:, k % X_RING, :], h_hi[:, k, :].bitcast(F32), ALU.subtract)\
                .then_inc(h_ready[0], 1)

        dve.wait_ge(pair_read[3], READ_GB)
        for k in range(KT):
            dve.wait_ge(x_in[k % X_RING], 32 + 16 * (k // X_RING + 1))
            nc.vector.scalar_tensor_tensor(x_raw[:, k % X_RING, :], x_raw[:, k % X_RING, :], g_col(k), factors[:, :],
                                           ALU.mult, ALU.mult).then_inc(h_scaled, 1)
            if k == 1:
                scaled_gate(0)
                split_lo(0, 4)
            if k % 2:
                h_low(k - 1)
        split_lo(0, 5)
        for j in range(1, 4):
            scaled_gate(j)
        for j in range(4):
            split_lo(0, 4 + j + 2)

        dve.wait_ge(gate_b_out, 16 * KT)
        nc.vector.memset(u_pad[:, 0:CONV - 1], 0.0)
        with dve.Fori(0, KT) as c:
            def step(n):
                return CONV_STEPS * c + (CONV_STEPS + n)

            def conv_col(n):
                return cols[:, bass.ds(c + (1 + n) * KT, 1)]

            split_lo(4 * c, CONV_0 + 2)
            split_lo(4 * c, CONV_0 + 3)
            dve.wait_ge(pair_read[0], c + (READ_CONV + 1))
            dve.wait_ge(block_done, 4 * c + (RING + CONV_0 + 2))
            nc.vector.tensor_tensor(u_pad[:, CONV - 1:], pair(1), u_pad[:, CONV - 1:], ALU.mult)\
                .then_inc(pair_read[1], 1)
            dve.wait_ge(pair_read[1], c + (READ_CONV + 1))
            nc.vector.tensor_scalar(taps[:, :], u_pad[:, 0:T], conv_col(0), conv_col(CONV), ALU.mult, ALU.add)\
                .then_inc(conv_step, 1)
            for n in range(1, CONV):
                dve.wait_ge(conv_step, step(n))
                nc.vector.scalar_tensor_tensor(taps[:, :], u_pad[:, n:n + T], conv_col(n), taps[:, :],
                                               ALU.mult, ALU.add).then_inc(conv_step, 1)
            split_lo(4 * c, CONV_0 + 4)
            dve.wait_ge(sig_c_ready, c + 1)
            nc.vector.tensor_tensor(gate_zb[:, :], pair(2), gate_zb[:, :], ALU.mult)\
                .then_inc(pair_read[2], 1)
            split_lo(4 * c, CONV_0 + 5)
            dve.wait_ge(block_done, 4 * c + (RING + CONV_0 + 4))
            dve.wait_ge(pair_read[2], c + (READ_CONV + 1))
            nc.vector.tensor_tensor(gate_zb[:, :], pair(3), gate_zb[:, :], ALU.mult)\
                .then_inc(pair_read[3], 1)
            dve.wait_ge(pair_read[3], c + (READ_CONV + 1))
            dve.wait_ge(conv_step, step(3))
            nc.vector.tensor_tensor(taps[:, :], gate_zb[:, :], taps[:, :], ALU.mult).then_inc(conv_step, 1)
            dve.wait_ge(conv_step, step(4))
            nc.vector.tensor_scalar(y_hi[:, c, :], taps[:, :], 1.0, None, ALU.mult).then_inc(conv_step, 1)
            dve.wait_ge(conv_step, step(5))
            nc.vector.tensor_tensor(y_lo[:, c, :], taps[:, :], y_hi[:, c, :].bitcast(F32), ALU.subtract)\
                .then_inc(y_ready, 1)

        with dve.Fori(0, KT // 2) as i:
            for j in (1, 3):
                split_lo(4 * i, MIX_0 + j + 1)
                split_lo(4 * i, MIX_0 + j + 2)
                dve.wait_ge(block_done, 4 * i + (RING + MIX_0 + j + 1))
                dve.wait_ge(pair_read[j - 1], i + (READ_MIX + 1))
                dve.wait_ge(mixed_out, 32 * i + 32)
                nc.vector.tensor_tensor(mixed_a[:, j // 2, :], pair(j), sig_a[:, j // 2, :], ALU.mult)\
                    .then_inc(pair_read[j], 1)

        def rotate(h, j):
            lo, hi = ((q_lo, q_hi), (k_lo, k_hi))[j]
            cos, sin = rope_sb[:, 0, :], rope_sb[:, 1, :]
            one, two = pair(2 * j), pair(2 * j + 1)
            at = 2 * TURN_STEPS * h + TURN_STEPS * (1 + j)
            dve.wait_ge(block_done, HEAD_BLOCKS * h + (RING + HEAD_0 + 2 * j + 2))
            dve.wait_ge(turn_step, at)
            nc.vector.tensor_tensor(turn_1[:, :], one, cos, ALU.mult).then_inc(turn_step, 1)
            nc.vector.tensor_tensor(turn_2[:, :], two, sin, ALU.mult).then_inc(turn_step, 1)
            dve.wait_ge(turn_step, at + 2)
            nc.vector.tensor_tensor(turn_1[:, :], turn_1[:, :], turn_2[:, :], ALU.subtract).then_inc(turn_step, 1)
            dve.wait_ge(turn_step, at + 3)
            nc.vector.tensor_tensor(turn_2[:, :], one, sin, ALU.mult)\
                .then_inc(pair_read[2 * j], 1)
            dve.wait_ge(turn_hi_ready, 4 * h + (2 * j + 1))
            nc.vector.tensor_tensor(lo[:, 0, :], turn_1[:, :], hi[:, 0, :].bitcast(F32), ALU.subtract)\
                .then_inc(turn_step, 1)
            dve.wait_ge(turn_step, at + 4)
            nc.vector.tensor_tensor(turn_1[:, :], two, cos, ALU.mult)\
                .then_inc(pair_read[2 * j + 1], 1)
            for n in (2 * j, 2 * j + 1):
                dve.wait_ge(pair_read[n], head_read(n, h, 1))
            nc.vector.tensor_tensor(turn_2[:, :], turn_2[:, :], turn_1[:, :], ALU.add).then_inc(turn_step, 1)
            dve.wait_ge(turn_hi_ready, 4 * h + (2 * j + 2))
            nc.vector.tensor_tensor(lo[:, 1, :], turn_2[:, :], hi[:, 1, :].bitcast(F32), ALU.subtract)\
                .then_inc(turn_step, 1)

        def score(h, n):
            at = psum[:, n % 2, :]
            dve.wait_ge(bank_full[n % 2], full_head(0, h, 1 + n // 2))
            if n < TT - 1:
                nc.vector.tensor_scalar(at[:, P:P + QK], at[:, P:P + QK], key_decay, None, ALU.mult)
            nc.vector.tensor_tensor(at[:, 0:P], at[:, 0:P], decay, ALU.mult).then_inc(score_made, 1)
            parts = 2 if n < TT - 1 else 1
            dve.wait_ge(score_hi_ready, (2 * TT - 1) * h + (2 * n + parts))
            if n < TT - 1:
                nc.vector.tensor_tensor(key_lo[:, n % 2, :], at[:, P:P + QK], key_hi[:, n % 2, :].bitcast(F32),
                                        ALU.subtract)
            nc.vector.tensor_tensor(score_lo[:, n % 2, :], at[:, 0:P], score_hi[:, n % 2, :].bitcast(F32),
                                    ALU.subtract).then_inc(pair_read[0], 1)

        def new_state(h, n):
            for b in (2, 3):
                dve.wait_ge(bank_full[b], full_head(b, h, 1 + n))
            if n == 0:
                made = nc.vector.tensor_copy(state[:, :], pair(1))
            else:
                dve.wait_ge(state_ready, (TT - 1) * h + n)
                made = nc.vector.scalar_tensor_tensor(state[:, :], state[:, :], chunk_decay, pair(1), ALU.mult, ALU.add)
            made.then_inc(pair_read[1], 1)

        def state_low(h, n):
            dve.wait_ge(state_hi_ready, (TT - 1) * h + (n + 1))
            nc.vector.tensor_tensor(state_lo[:, n % 2, :], state[:, :], state_hi[:, n % 2, :].bitcast(F32),
                                    ALU.subtract).then_inc(state_ready, 1)

        with dve.Fori(0, HEADS) as h:
            for j in range(4):
                split_lo(HEAD_BLOCKS * h, HEAD_0 + j + 2)
                if j % 2:
                    dve.wait_ge(rope_in, 16 * h + 16)
                    rotate(h, j // 2)
            for s in range(4):
                split_lo(HEAD_BLOCKS * h, HEAD_0 + 4 + s + 2)
            for t in range(TT):
                dve.wait_ge(v_hi_ready, TT * h + (t + 1))
                nc.vector.tensor_tensor(v_lo[:, t, :], psum[:, t, :], v_hi[:, t, :].bitcast(F32), ALU.subtract)\
                    .then_inc(pair_read[t // 2], 1)
            dve.wait_ge(table_in, 16 * h + 16)
            score(h, 0)
            score(h, 1)

            def silu_product(m):
                at = (m % 2) * HALF
                if m % 2 == 0:
                    split_lo(HEAD_BLOCKS * h, HEAD_0 + SILU_0 + m // 2 + 2)
                dve.wait_ge(sig_z_ready, SILU_PARTS * h + (m + 1))
                nc.vector.tensor_tensor(silu_z[:, at:at + HALF], psum[:, 7, :], silu_z[:, at:at + HALF], ALU.mult)\
                    .then_inc(silu_read, 1)

            silu_product(0)
            new_state(h, 0)
            state_low(h, 0)
            for n in range(TT):
                if n + 2 < TT:
                    score(h, n + 2)
                if n + 1 < TT - 1:
                    new_state(h, n + 1)
                    state_low(h, n + 1)
                    silu_product(n + 1)
            silu_product(SILU_PARTS - 1)

        def split_o_lo(i, e):
            dve.wait_ge(o_hi_ready, 4 * i + (e + 1))
            nc.vector.tensor_tensor(o_lo[:, e % RING, :], o_raw[:, e % RING, :], o_hi[:, e % RING, :].bitcast(F32),
                                    ALU.subtract).then_inc(o_ready, 1)

        def gate_o(i, e):
            n = e % RING
            if e < RING:
                dve.wait_ge(first_back[n], 32)
            else:
                dve.wait_ge(o_back[n], 16 * i + 16 * (e // RING))
                dve.wait_ge(silu_back[n], 16 * i + 16 * (e // RING))
            nc.vector.tensor_tensor(o_raw[:, n, :], o_raw[:, n, :], silu_raw[:, n, :], ALU.mult).then_inc(o_gated, 1)

        gate_o(0, 0)
        gate_o(0, 1)
        split_o_lo(0, 0)
        split_o_lo(0, 1)
        for half in range(2):
            first, e0 = LAST_0 + half * HALF_BLOCKS, half * YB_BLOCKS
            for j in range(2):
                gate_o(0, e0 + j + 2)
                split_lo(0, first + j + 2)
                split_o_lo(0, e0 + j + 2)
            with dve.Fori(0, YB_BLOCKS // RING - 1) as i:
                for j in range(2, 2 + RING):
                    gate_o(i, e0 + j + 2)
                    split_lo(4 * i, first + j + 2)
                    split_o_lo(i, e0 + j + 2)
            for j in range(YB_BLOCKS - 2, YB_BLOCKS):
                split_lo(0, first + j + 2)
            dve.wait_ge(gates_back, 32 * (half + 1))
            n0 = half * KT

            def gated(k):
                if k < BANKS - 1:
                    dve.wait_ge(bank_full[k], full_last(k, half, 0))
                else:
                    dve.wait_ge(block_done, RING + first + YB_BLOCKS)
                nc.vector.tensor_tensor(merged[:, k, :], psum[:, k, :], gate_b_in[:, k, :], ALU.mult)\
                    .then_inc(pair_read[k // 2], 1)

            def add_mixed(k):
                dve.wait_ge(pair_read[k // 2], last_read(k // 2, half, k % 2 + 1))
                nc.vector.tensor_tensor(merged[:, k, :], merged[:, k, :], mixed_in[:, k, :], ALU.add)\
                    .then_inc(merged_ready, 1)

            def merged_lo(k):
                dve.wait_ge(m_hi_ready, n0 + k + 1)
                nc.vector.tensor_tensor(m_lo[:, k, :], merged[:, k, :], m_hi[:, k, :].bitcast(F32), ALU.subtract)\
                    .then_inc(m_ready, 1)

            gated(0)
            gated(1)
            add_mixed(0)
            gated(2)
            merged_lo(0)
            for k in range(3, KT):
                gated(k)
            for k in range(1, KT):
                add_mixed(k)
                if first + YB_BLOCKS + k + 1 < STREAM:
                    split_lo(0, first + YB_BLOCKS + k + 1)
                merged_lo(k)
            if half == 0:
                split_lo(0, first + YB_BLOCKS + OUT_BLOCKS + 1)
                gate_o(0, YB_BLOCKS)
                gate_o(0, YB_BLOCKS + 1)
                split_o_lo(0, YB_BLOCKS)
                split_o_lo(0, YB_BLOCKS + 1)
            dve.wait_ge(result_in, 16 * (half + 1))
            dve.wait_ge(final_in, 16)

            def add_x(t):
                dve.wait_ge(bank_full[2 * t], full_last(2 * t, half, 1))
                if t < OUT_TILES - 1:
                    dve.wait_ge(bank_full[2 * t + 1], full_last(2 * t + 1, half, 1))
                else:
                    dve.wait_ge(block_done, RING + first + HALF_BLOCKS)
                nc.vector.tensor_tensor(result[:, t, :], pair(t), result[:, t, :], ALU.add)\
                    .then_inc(pair_read[t], 1)

            def normed(t):
                dve.wait_ge(last_scale_ready, half * OUT_TILES + t + 1)
                nc.vector.scalar_tensor_tensor(result[:, t, :], result[:, t, :], rms_scale[:, t % 2:t % 2 + 1],
                                               final_sb[:, :], ALU.mult, ALU.mult).then_inc(result_ready, 1)

            add_x(0)
            for t in range(1, OUT_TILES):
                add_x(t)
                normed(t - 1)
            normed(OUT_TILES - 1)

    @block.tensor
    def _(pe):
        def product(dst, left, right, start, stop, l=slice(None), r=slice(None)):
            (l_hi, l_lo), (r_hi, r_lo) = left, right
            nc.tensor.matmul(dst, l_hi, r_hi, start=start, stop=False)
            nc.tensor.matmul(dst, l_hi, r_lo, start=False, stop=False)
            return nc.tensor.matmul(dst, l_lo, r_hi, start=False, stop=stop)

        def channel_block(b, n, j, read, hi, lo, arrived=None, midway=None):
            pe.wait_ge(parts_ready, b + (n + 1))
            pe.wait_ge(pair_read[j], read)
            slot = n % RING
            for k in range(KT):
                if arrived:
                    pe.wait_ge(*arrived(k))
                if midway and k == KT // 2:
                    midway()
                w = slice(k * P, (k + 1) * P)
                for part in range(2):
                    t = slice(part * BANK, (part + 1) * BANK)
                    last = product(psum[:, 2 * j + part, :], (w_hi[:, slot, w], w_lo[:, slot, w]),
                                   (hi[:, k, t], lo[:, k, t]), k == 0, k == KT - 1)
            last.then_inc(block_done, 1)

        def row_blocks(b, n, read):
            for s in range(4):
                pe.wait_ge(parts_ready, b + (n + s + 1))
                slot = (n + s) % RING
                groups = 2 if s == 0 else 1
                for kk, t in ((kk, t) for g in range(groups) for kk in range(2)
                              for t in range(g * TT // groups, (g + 1) * TT // groups)):
                    k = 2 * s + kk
                    if k == 0 and t % 2 == 0:
                        pe.wait_ge(pair_read[t // 2], read(t // 2))
                    rows, c = slice(t * P, (t + 1) * P), slice(kk * V, (kk + 1) * V)
                    last = product(psum[:, t, :], (h_hi[:, k, rows], h_lo[:, k, rows]),
                                   (w_hi[:, slot, c], w_lo[:, slot, c]), k == 0, k == KT - 1)
                    if k == KT - 1 and t < BANKS - 1:
                        last.then_inc(bank_full[t], 1)
                last.then_inc(block_done, 1)

        pe.sem_inc(block_done, RING)

        def spread_factors():
            pe.wait_ge(pool_consts, 3)
            for part in range(2):
                pe.wait_ge(diag_ready, (part + 1) * TT // 2)
                nc.tensor.matmul(psum[:, 6 + part, :], ones[:, :],
                                 diagonal[:, part * TT // 2:(part + 1) * TT // 2, :].rearrange("p t n -> p (t n)"),
                                 start=True, stop=True).then_inc(factors_full, 1)

        for j in range(4):
            channel_block(0, j, j, READ_GB, xg_hi, xg_lo, (lambda k: (xg_ready, k + 1)) if j == 0 else None,
                          spread_factors if j == 2 else None)
        for j in range(4):
            channel_block(0, 4 + j, j, READ_GB + 1, h_hi, h_lo,
                          (lambda k: (h_ready[k % 2], k // 2 + 1)) if j == 0 else None)

        with pe.Fori(0, KT) as c:
            for j in range(4):
                channel_block(4 * c, CONV_0 + j, j, c + READ_CONV, h_hi, h_lo)

        with pe.Fori(0, KT // 2) as i:
            for j in range(4):
                if j == 1:
                    pe.wait_ge(y_ready, KT)
                hi, lo = (y_hi, y_lo) if j % 2 else (h_hi, h_lo)
                channel_block(4 * i, MIX_0 + j, j, i + READ_MIX, hi, lo)

        def chunk(n):
            return slice(n * P, (n + 1) * P)

        def scores(h, n):
            bank = n % 2
            pe.wait_ge(pair_read[0], head_read(0, h, 3 + max(n - 1, 0)))
            for d in range(DQ):
                last = product(psum[:, bank, 0:P], (k_hi[:, d, chunk(n)], k_lo[:, d, chunk(n)]),
                               (q_hi[:, d, chunk(n)], q_lo[:, d, chunk(n)]), d == 0, d == DQ - 1)
            if n < TT - 1:
                for d in range(DQ):
                    to = psum[:, bank, P + d * P:P + (d + 1) * P]
                    nc.tensor.matmul(to, k_hi[:, d, chunk(n)], ident_r[:, :], start=True, stop=False)
                    last = nc.tensor.matmul(to, k_lo[:, d, chunk(n)], ident_r[:, :], start=False, stop=True)
            last.then_inc(bank_full[bank], 1)

        def update(h, n):
            pe.wait_ge(pair_read[0], ret_read(0, h, n))
            pe.wait_ge(pair_read[1], head_read(1, h, 3 + n))
            for d in range(DQ):
                c = slice(d * P, (d + 1) * P)
                product(psum[:, 2 + d, :], (key_hi[:, n % 2, c], key_lo[:, n % 2, c]),
                        (v_hi[:, n, :], v_lo[:, n, :]), True, True).then_inc(bank_full[2 + d], 1)

        def rows(h, n):
            bank = 4 + n % 2
            pe.wait_ge(pair_read[2], head_read(2, h, 3 + max(n - 1, 0)))
            pe.wait_ge(pair_read[0], ret_read(0, h, n))
            last = product(psum[:, bank, :], (score_hi[:, n % 2, :], score_lo[:, n % 2, :]),
                           (v_hi[:, n, :], v_lo[:, n, :]), True, n == 0)
            if n:
                pe.wait_ge(state_ready, (TT - 1) * h + n)
                for d in range(DQ):
                    c = slice(d * V, (d + 1) * V)
                    last = product(psum[:, bank, :], (q_hi[:, d, chunk(n)], q_lo[:, d, chunk(n)]),
                                   (state_hi[:, (n - 1) % 2, c], state_lo[:, (n - 1) % 2, c]), False, d == DQ - 1)
            last.then_inc(bank_full[bank], 1)

        def transposed(h, n):
            bank = 6
            pe.wait_ge(pair_read[3], head_read(3, h, 3 + n))
            pe.wait_ge(pair_read[2], ret_read(2, h, n))
            for e in range(ET):
                last = nc.tensor.transpose(psum[:, bank, e * P:(e + 1) * P], o_rows[:, e * P:(e + 1) * P], ident[:, :])
            last.then_inc(bank_full[bank], 1)

        pe.wait_ge(ident_ready, 1)
        with pe.Fori(0, HEADS) as h:
            for j in range(4):
                if j == 3:
                    pe.wait_ge(silu_read, SILU_PARTS * h + SILU_PARTS)
                channel_block(HEAD_BLOCKS * h, HEAD_0 + j, j, head_read(j, h, 0), h_hi, h_lo)
            row_blocks(HEAD_BLOCKS * h, HEAD_0 + 4, lambda j: head_read(j, h, 1))
            pe.wait_ge(turn_step, 2 * TURN_STEPS * h + 3 * TURN_STEPS)
            scores(h, 0)
            scores(h, 1)

            def silu_part(m):
                n, t = HEAD_0 + SILU_0 + m // 2, slice((m % 2) * HALF, (m % 2 + 1) * HALF)
                pe.wait_ge(parts_ready, HEAD_BLOCKS * h + (n + 1))
                if m:
                    pe.wait_ge(silu_read, SILU_PARTS * h + (SILU_PARTS + m))
                for k in range(KT):
                    w = slice(k * P, (k + 1) * P)
                    last = product(psum[:, 7, :], (w_hi[:, n % RING, w], w_lo[:, n % RING, w]),
                                   (h_hi[:, k, t], h_lo[:, k, t]), k == 0, k == KT - 1)
                last.then_inc(block_done if m % 2 else bank_full[7], 1)

            for j in range(BANKS // 2):
                pe.wait_ge(pair_read[j], head_read(j, h, 3))
            silu_part(0)
            update(h, 0)
            for n in range(TT):
                if n + 2 < TT:
                    scores(h, n + 2)
                rows(h, n)
                if n + 1 < TT - 1:
                    update(h, n + 1)
                    silu_part(n + 1)
                if n:
                    transposed(h, n - 1)
            silu_part(SILU_PARTS - 1)
            transposed(h, TT - 1)

        def o_block(i, half, e, start, stop):
            n = LAST_0 + half * HALF_BLOCKS + e
            pe.wait_ge(parts_ready, 4 * i + (n + 1))
            pe.wait_ge(o_ready, 4 * i + (half * YB_BLOCKS + e + 1))
            slot = e % RING
            for d in range(KT):
                if start and d % 2 == 0:
                    pe.wait_ge(pair_read[d // 2], last_read(d // 2, half, 0))
                if start and d == 7:
                    pe.wait_ge(silu_read, SILU_PARTS * (HEADS + 1))
                w = slice(d * P, (d + 1) * P)
                last = product(psum[:, d, :], (w_hi[:, n % RING, w], w_lo[:, n % RING, w]),
                               (o_hi[:, slot, :], o_lo[:, slot, :]), start, stop)
                if stop and d < BANKS - 1:
                    last.then_inc(bank_full[d], 1)
            last.then_inc(block_done, 1)

        for half in range(2):
            for e in range(RING):
                o_block(0, half, e, e == 0, False)
            with pe.Fori(0, YB_BLOCKS // RING - 2) as i:
                for e in range(RING, 2 * RING):
                    o_block(i, half, e, False, False)
            for e in range(YB_BLOCKS - RING, YB_BLOCKS):
                o_block(0, half, e, False, e == YB_BLOCKS - 1)
            for k in range(OUT_BLOCKS):
                n = LAST_0 + half * HALF_BLOCKS + YB_BLOCKS + k
                pe.wait_ge(parts_ready, n + 1)
                pe.wait_ge(m_ready, half * KT + k + 1)
                for t in range(OUT_TILES):
                    for c in range(2):
                        bank = 2 * t + c
                        if k == 0 and c == 0:
                            pe.wait_ge(pair_read[t], last_read(t, half, 2))
                        left = (m_hi[:, k, chunk(t)], m_lo[:, k, chunk(t)])
                        w = slice(c * BANK, (c + 1) * BANK)
                        last = product(psum[:, bank, :], left, (w_hi[:, n % RING, w], w_lo[:, n % RING, w]),
                                       k == 0, k == OUT_BLOCKS - 1)
                        if k == OUT_BLOCKS - 1 and bank < BANKS - 1:
                            last.then_inc(bank_full[bank], 1)
                last.then_inc(block_done, 1)

    held.close()


def weight_stream(w_in, w_a, w_b, w_o):
    def channels(w, c0):
        return w[:, c0:c0 + P].reshape(KT, P, P).transpose(1, 0, 2).reshape(P, BLOCK)

    def columns(w, c0):
        return [w[2 * s * P:(2 * s + 2) * P, c0:c0 + V].reshape(2, P, V).transpose(1, 0, 2).reshape(P, BLOCK)
                for s in range(4)]

    b0, c0, x0, z0, q0, k0 = (n * D for n in range(6))
    v0, zb0, ga0, gb0 = 6 * D, 8 * D, 10 * D, 11 * D
    blocks = [channels(w_in, gb0 + d * P) for d in range(KT)]
    for c in range(KT):
        blocks += [channels(w_in, at + c * P) for at in (c0, x0, z0, b0)]
    for d in range(KT):
        blocks += [channels(w_in, ga0 + d * P), channels(w_a, d * P)]
    for h in range(HEADS):
        blocks += [channels(w_in, at + h * QK + d * P) for at in (q0, k0) for d in range(DQ)]
        blocks += columns(w_in, v0 + h * V)
        blocks += [channels(w_in, zb0 + h * V + e * P) for e in range(ET)]
    ends = [w_b[e * P:(e + 1) * P] for e in range(YB_BLOCKS)] + [w_o[k * P:(k + 1) * P] for k in range(OUT_BLOCKS)]
    return np.ascontiguousarray(np.stack(blocks + ends + ends))


def kernel(x, norm_g, w_in, conv_w, conv_b, w_a_out, w_b_out, w_o, final_g):
    import concourse.bacc as bacc
    from concourse.bass_utils import run_bass_kernel_spmd

    x2 = np.asarray(x)[0]
    rope, table, identity = constants()
    per_tile = [np.asarray(norm_g)[0], *np.asarray(conv_w)[0], np.asarray(conv_b)[0]]
    arrays = {
        "x_t": np.ascontiguousarray(x2.T.reshape(KT, P, T)),
        "x_rows": np.ascontiguousarray(x2.reshape(TT, P, D)),
        "columns": np.ascontiguousarray(np.concatenate([a.reshape(KT, P).T for a in per_tile], axis=1)),
        "weights": weight_stream(*(np.asarray(w)[0] for w in (w_in, w_a_out, w_b_out, w_o))),
        "final_g": np.ascontiguousarray(np.broadcast_to(np.asarray(final_g), (P, D))),
        "rope": rope,
        "head_table": table,
        "identity": identity,
    }
    nc = bacc.Bacc("TRN2", target_bir_lowering=False, num_devices=1)
    aps = [nc.dram_tensor(name, a.shape, mybir.dt.from_np(a.dtype), kind="ExternalInput").ap()
           for name, a in arrays.items()]
    out = nc.dram_tensor("out", (TT, P, D), F32, kind="ExternalOutput").ap()
    build(nc, *aps, out)
    r = run_bass_kernel_spmd(nc, [arrays], core_ids=[0])
    return r.results[0]["out"].reshape(1, T, D)
```

```python
from contextlib import ExitStack

import numpy as np
import concourse.bass as bass
from concourse import mybir

F32 = mybir.dt.float32
F32R = mybir.dt.float32r
BF16 = mybir.dt.bfloat16
ACT = mybir.ActivationFunctionType
ALU = mybir.AluOpType

P = 128
D = 1024
T = 1024
KT = D // P
TT = T // P
BANK = 512
BANKS = 8
BLOCK = 1024
HEADS = 4
QK = D // HEADS
DQ = QK // P
V = 2 * D // HEADS
ET = V // P
CHUNK = P
EPS = 1e-6
HALF = T // 2
CONV = 3
RING = 4
RAW = 2
FIRST, SECOND = slice(0, BLOCK // 2), slice(BLOCK // 2, BLOCK)
X_RING = 4
WARM_UP = 12

GB_BLOCKS, CONV_BLOCKS, MIX_BLOCKS = KT - 1, 4 * KT, 2 * KT
HEAD_BLOCKS, YB_BLOCKS, OUT_BLOCKS = 8 + ET, HEADS * ET, KT
SILU_0 = 8
CONV_0 = GB_BLOCKS
MIX_0 = CONV_0 + CONV_BLOCKS
HEAD_0 = MIX_0 + MIX_BLOCKS
LAST_GATE = HEAD_0 + HEADS * HEAD_BLOCKS
LAST_0 = LAST_GATE + 1
HALF_BLOCKS = YB_BLOCKS + OUT_BLOCKS
STREAM = LAST_0 + 2 * HALF_BLOCKS

READ_GB = 1
READ_CONV = READ_GB + KT // 4
READ_MIX = READ_CONV + KT
READ_HEAD = READ_MIX + MIX_BLOCKS // 4
HEAD_READS = [n + 3 for n in (TT, TT - 1, TT, TT)]
SILU_PARTS = 2 * ET
SILU_AFTER = {0: 1, 1: 2, 2: 3, 3: 4, 4: 5, TT - 2: 6}


def head_read(j, h, n):
    return HEAD_READS[j] * h + (READ_HEAD + n)


def ret_read(j, h, n):
    return head_read(j, h, 3 + n + 1)


def last_read(j, half, n):
    return READ_HEAD + HEADS * HEAD_READS[j] + (j == 2) + 3 * half + n


def full_head(bank, h, n):
    uses = [TT // 2, TT // 2, TT - 1, TT - 1, TT // 2, TT // 2, SILU_PARTS // 2, TT][bank]
    return uses * h + n if bank == 7 else (1 + uses) * h + (n + 1)


def full_last(bank, half, n):
    return full_head(bank, HEADS, 0) + 2 * half + n


def constants():
    freq = (10000.0 ** (-(np.arange(0, QK, 2, dtype=np.float32) / np.float32(QK)).astype(np.float64)))
    freq = freq.astype(np.float32)
    angle = (np.arange(T, dtype=np.float32)[None, :] * freq[:, None]).astype(np.float64)
    rope = np.stack([np.cos(angle), np.sin(angle)]).astype(np.float32)
    table = np.zeros((HEADS, P, P + 4), np.float64)
    j = np.arange(P, dtype=np.float64)
    for h in range(HEADS):
        gamma = 1.0 - 2.0 ** (-5.0 - h)
        xi = gamma ** (j + 1)
        table[h, :, :P] = (j[None, :] >= j[:, None]) * (gamma ** -(j + 1))[:, None] * QK ** -0.5
        table[h, :, P] = gamma ** (CHUNK - 1 - j) * QK ** -0.5
        table[h, :, P + 1] = xi / np.sqrt(V)
        table[h, :, P + 2] = xi
        table[h, :, P + 3] = gamma ** CHUNK
    return rope, table.astype(np.float32), np.eye(P, dtype=np.float32)


def build(nc, x_t, x_rows, columns, weights, final_g, rope, head_table, identity, out):
    gate_b_d = nc.dram_tensor("gate_b_scratch", (KT, P, T), F32, kind="Internal").ap()
    mixed_a_d = nc.dram_tensor("mixed_a_scratch", (KT, P, T), F32, kind="Internal").ap()
    silu_d = nc.dram_tensor("silu_scratch", (HEADS * ET, P, T), F32, kind="Internal").ap()
    o_d = nc.dram_tensor("o_scratch", (2, HEADS * ET, P, HALF), F32, kind="Internal").ap()

    held = ExitStack()

    def sb(stack, name, shape, dt):
        return stack.enter_context(nc.sbuf_tensor(name, shape, dt))

    def sem(name):
        return held.enter_context(nc.semaphore(name))

    w_hi = sb(held, "w_hi", [P, RING, BLOCK], F32R)
    w_lo = sb(held, "w_lo", [P, RING, BLOCK], F32R)
    w_raw = sb(held, "w_raw", [P, RAW, BLOCK], F32)
    ident = sb(held, "ident", [P, P], F32)
    NCOL = KT * (2 + CONV)
    cols = sb(held, "cols", [P, NCOL], F32)
    small = sb(held, "small", [P, 4 * TT + 2], F32)
    rms_var, rms_scale, minus_half = (small[:, n * TT:(n + 1) * TT] for n in range(3))
    square_sum = small[:, 3 * TT:4 * TT]
    eps, unused_col = small[:, 4 * TT:4 * TT + 1], small[:, 4 * TT + 1:4 * TT + 2]
    psum = held.enter_context(nc.psum_tensor("psum", [P, BANKS, BANK], F32))

    def g_col(k):
        return cols[:, k:k + 1]

    with ExitStack() as s:
        rows_raw = sb(s, "rows_raw", [P, TT, D], F32)
        diagonal = sb(s, "diagonal", [P, TT, P], F32)
        ones = sb(s, "ones", [P, P], F32)
    with ExitStack() as upper:
        h_hi = sb(upper, "h_hi", [P, KT, T], F32R)
        h_lo = sb(upper, "h_lo", [P, KT, T], F32R)
        with ExitStack() as s:
            xg_hi = sb(s, "xg_hi", [P, KT, T], F32R)
            xg_lo = sb(s, "xg_lo", [P, KT, T], F32R)
            x_raw = sb(s, "x_raw", [P, X_RING, T], F32)
            gate_b = sb(s, "gate_b", [P, 4, T], F32)
            factors = sb(s, "factors", [P, T], F32)
        with ExitStack() as s:
            y_hi = sb(s, "y_hi", [P, KT, T], F32R)
            y_lo = sb(s, "y_lo", [P, KT, T], F32R)
            with ExitStack() as s2:
                u_pad = sb(s2, "u_pad", [P, T + CONV - 1], F32)
                taps = sb(s2, "taps", [P, T], F32)
                gate_zb = sb(s2, "gate_zb", [P, T], F32)
            with ExitStack() as s2:
                sig_a = sb(s2, "sig_a", [P, 2, T], F32)
                mixed_a = sb(s2, "mixed_a", [P, 2, T], F32)
        with ExitStack() as s:
            k_hi = sb(s, "k_hi", [P, DQ, T], F32R)
            k_lo = sb(s, "k_lo", [P, DQ, T], F32R)
            with ExitStack() as s2:
                rope_sb = sb(s2, "rope_sb", [P, 2, T], F32)
                turn = sb(s2, "turn", [P, 4, T], F32)
            v_parts = sb(s, "v_parts", [P, TT, 2, V], F32R)
            q_hi = sb(s, "q_hi", [P, TT, DQ + 1, P], F32R)
            q_lo = sb(s, "q_lo", [P, DQ, T], F32R)
            state_hi = sb(s, "state_hi", [P, 2, DQ * V], F32R)
            state_lo = sb(s, "state_lo", [P, 2, DQ * V], F32R)
            score_hi = sb(s, "score_hi", [P, 2, P], F32R)
            score_lo = sb(s, "score_lo", [P, 2, P], F32R)
            key_hi = sb(s, "key_hi", [P, 2, QK], F32R)
            key_lo = sb(s, "key_lo", [P, 2, QK], F32R)
            scored = sb(s, "scored", [P, P], F32)
            state = sb(s, "state", [P, DQ * V], F32)
            o_t = sb(s, "o_t", [P, ET, P], F32)
            o_rows = sb(s, "o_rows", [P, V], F32)
            table = sb(s, "table", [P, P + 4], F32)
            unused = sb(s, "unused", [P, V], BF16)
            silu_z = sb(s, "silu_z", [P, HALF], F32)
    with ExitStack() as last:
        m_hi = sb(last, "m_hi", [P, KT, HALF], F32R)
        m_lo = sb(last, "m_lo", [P, KT, HALF], F32R)
        merged = sb(last, "merged", [P, KT, HALF], F32)
        result = sb(last, "result", [P, 4, D], F32)
        o_hi = sb(last, "o_hi", [P, RING, HALF], F32R)
        o_lo = sb(last, "o_lo", [P, RING, HALF], F32R)
        o_raw = sb(last, "o_raw", [P, RING, HALF], F32)
        silu_raw = sb(last, "silu_raw", [P, RING, HALF], F32)
        gate_b_in = sb(last, "gate_b_in", [P, KT, HALF], F32)
        mixed_in = sb(last, "mixed_in", [P, KT, HALF], F32)
        final_sb = sb(last, "final_sb", [P, D], F32)
        unused_last = sb(last, "unused_last", [P, D], BF16)

    v_hi, v_lo = v_parts[:, :, 0, :], v_parts[:, :, 1, :]
    decay, key_decay, xi_mean, xi, chunk_decay = (
        table[:, 0:P], table[:, P:P + 1], table[:, P + 1:P + 2], table[:, P + 2:P + 3], table[:, P + 3:P + 4])

    last_gate = state

    raw_in = [sem(f"raw_in{n}") for n in range(RAW)]
    hi_ready = sem("hi_ready")
    parts_ready = sem("parts_ready")
    block_done = sem("block_done")
    bank_full = [sem(f"bank_full{b}") for b in range(BANKS)]
    pair_read = [sem(f"pair_read{j}") for j in range(BANKS // 2)]
    consts_in = sem("consts_in")
    ident_in = sem("ident_in")
    x_in = [sem(f"x_in{n}") for n in range(X_RING)]
    x_first_in = sem("x_first_in")
    w_first_in = [sem(f"w_first_in{n}") for n in range(2)]
    first_hi = sem("first_hi")
    first_ready = sem("first_ready")
    rows_in = [sem(f"rows_in{t}") for t in range(TT)]
    pool_consts = sem("pool_consts")
    beside_q = sem("beside_q")
    xg_hi_ready = sem("xg_hi_ready")
    xg_ready = sem("xg_ready")
    squares_ready = sem("squares_ready")
    var_ready = sem("var_ready")
    rms_ready = sem("rms_ready")
    diag_ready = sem("diag_ready")
    factors_full = sem("factors_full")
    h_scaled = sem("h_scaled")
    h_hi_ready = sem("h_hi_ready")
    h_ready = [sem(f"h_ready{n}") for n in range(2)]
    gate_b_ready = sem("gate_b_ready")
    gate_b_out = sem("gate_b_out")
    sig_c_ready = sem("sig_c_ready")
    conv_step = sem("conv_step")
    y_ready = sem("y_ready")
    mixed_out = sem("mixed_out")
    rope_in = sem("rope_in")
    turn_step = sem("turn_step")
    turn_hi_ready = sem("turn_hi_ready")
    v_hi_ready = sem("v_hi_ready")
    table_in = sem("table_in")
    sig_z_ready = sem("sig_z_ready")
    silu_read = sem("silu_read")
    silu_out = sem("silu_out")
    score_decayed = sem("score_decayed")
    score_made = sem("score_made")
    score_hi_ready = sem("score_hi_ready")
    state_hi_ready = sem("state_hi_ready")
    state_ready = sem("state_ready")
    o_square_ready = sem("o_square_ready")
    o_var_ready = sem("o_var_ready")
    o_scale_ready = sem("o_scale_ready")
    o_out = sem("o_out")
    o_back = [sem(f"o_back{n}") for n in range(RING)]
    first_back = [sem(f"first_back{n}") for n in range(RING)]
    silu_back = [sem(f"silu_back{n}") for n in range(RING)]
    o_gated = sem("o_gated")
    o_hi_ready = sem("o_hi_ready")
    o_ready = sem("o_ready")
    gates_back = sem("gates_back")
    merged_ready = sem("merged_ready")
    m_hi_ready = sem("m_hi_ready")
    m_ready = sem("m_ready")
    result_in = sem("result_in")
    final_in = sem("final_in")
    last_square_ready = sem("last_square_ready")
    last_total_ready = sem("last_total_ready")
    last_var_ready = sem("last_var_ready")
    last_scale_ready = sem("last_scale_ready")
    result_ready = sem("result_ready")
    first_out = sem("first_out")
    result_out = sem("result_out")

    CONV_STEPS, TURN_STEPS = 5, 6
    OUT_TILES = HALF // P

    def pair(j):
        return psum[:, 2 * j:2 * j + 2, :].rearrange("p b n -> p (b n)")

    def by_chunk(a):
        return a.rearrange("p (n c) -> p n c", n=TT)

    block = held.enter_context(nc.Block())

    @block.sync
    def _(sp):
        def load_block(b, offset):
            n = offset + RAW + 2
            sp.wait_ge(parts_ready, b + (n - RAW + 1))
            sp.dma_start(w_raw[:, n % RAW, :], weights[b + n]).then_inc(raw_in[n % RAW], 16)

        sp.sem_inc(silu_out, 16)
        sp.sem_inc(mixed_out, 2 * 16)
        sp.sem_inc(o_out, 16)

        def load_x(n):
            sp.dma_start(x_raw[:, n % X_RING, :], x_t[n % KT]).then_inc(x_in[n % X_RING], 16)

        def load_rows(t):
            sp.dma_start(rows_raw[:, t, :], x_rows[t]).then_inc(rows_in[t], 16)

        sp.dma_start(cols[:, :], columns).then_inc(consts_in, 16)
        sp.dma_start(x_raw[:, 0, 0:HALF], x_t[0, :, 0:HALF]).then_inc(x_first_in, 16)
        sp.dma_start(w_raw[:, 0, FIRST], weights[0, :, FIRST]).then_inc(w_first_in[0], 16)
        sp.dma_start(x_raw[:, 0, HALF:T], x_t[0, :, HALF:T]).then_inc(x_in[0], 16)
        sp.dma_start(w_raw[:, 1, FIRST], weights[1, :, FIRST]).then_inc(w_first_in[1], 16)
        load_x(1)
        load_x(2)
        for n in range(2):
            sp.dma_start(w_raw[:, n, SECOND], weights[n, :, SECOND]).then_inc(raw_in[n], 16)
        load_x(3)
        for k in range(X_RING, KT):
            sp.wait_ge(xg_ready, k - X_RING + 1)
            load_x(k)
        sp.dma_start(ident[:, :], identity).then_inc(ident_in, 16)
        for t in range(TT // 2):
            load_rows(t)
        load_block(0, -2)
        for t in range(TT // 2, TT):
            load_rows(t)
        load_block(0, -1)
        for k in range(X_RING):
            sp.wait_ge(xg_ready, k + X_RING + 1)
            load_x(KT + k)
        load_block(0, 0)

        for k in range(X_RING, KT):
            sp.wait_ge(h_ready[k % 2], (k - X_RING) // 2 + 1)
            load_x(KT + k)
        for b in range(GB_BLOCKS):
            if b:
                load_block(0, b)
            if b < 4:
                sp.wait_ge(gate_b_ready, b + 1)
            else:
                sp.wait_ge(pair_read[b - 4], READ_GB + 2)
            sp.dma_start(gate_b_d[b], gate_b[:, b % 4, :]).then_inc(gate_b_out, 16)

        with sp.Fori(0, KT) as c:
            for j in range(4):
                load_block(4 * c, CONV_0 + j)

        with sp.Fori(0, KT // 2) as i:
            for j in range(4):
                load_block(4 * i, MIX_0 + j)
                if j % 2:
                    sp.wait_ge(pair_read[j], i + (READ_MIX + 1))
                    sp.dma_start(mixed_a_d[2 * i + j // 2], mixed_a[:, j // 2, :]).then_inc(mixed_out, 16)

        with sp.Fori(0, HEADS) as h:
            sp.wait_ge(o_out, 128 * h + 16)
            sp.wait_ge(silu_out, 128 * h + 16)
            sp.wait_ge(mixed_out, (2 + KT) * 16)
            sp.wait_ge(block_done, HEAD_BLOCKS * h + (RING + HEAD_0))
            sp.dma_start(rope_sb[:, :, :], rope.rearrange("c p t -> p c t")).then_inc(rope_in, 16)
            sp.dma_start(table[:, :], head_table[h]).then_inc(table_in, 16)

            def store_silu(m):
                sp.wait_ge(silu_read, SILU_PARTS * h + (SILU_PARTS + m + 1))
                at = (m % 2) * HALF
                sp.dma_start(silu_d[ET * h + m // 2, :, at:at + HALF], silu_z[:, :]).then_inc(silu_out, 16)

            def store_o(n):
                sp.wait_ge(pair_read[3], ret_read(3, h, n))
                at = (n % 4) * P
                sp.dma_start(o_d[n // 4].rearrange("(h e) p c -> h p e c", e=ET)[h, :, :, at:at + P],
                             o_t[:, :, :]).then_inc(o_out, 16)

            for j in range(SILU_0):
                load_block(HEAD_BLOCKS * h, HEAD_0 + j)
            store_silu(0)
            load_block(HEAD_BLOCKS * h, HEAD_0 + SILU_0)
            for n in range(TT):
                if n in SILU_AFTER:
                    store_silu(SILU_AFTER[n])
                if n:
                    store_o(n - 1)
                if SILU_AFTER.get(n, 1) % 2 == 0:
                    load_block(HEAD_BLOCKS * h, HEAD_0 + SILU_0 + SILU_AFTER[n] // 2)
            store_silu(SILU_PARTS - 1)
            store_o(TT - 1)

        load_block(0, LAST_GATE)
        sp.wait_ge(pair_read[2], last_read(2, 0, 0))
        sp.dma_start(gate_b_d[KT - 1], last_gate[:, :]).then_inc(gate_b_out, 16)

        def load_o(half, i, e):
            sp.dma_start(o_raw[:, e % RING, :], o_d[half, 4 * i + e]).then_inc(o_back[e % RING], 16)
            sp.dma_start(silu_raw[:, e % RING, :], silu_d[4 * i + e, :, half * HALF:(half + 1) * HALF])\
                .then_inc(silu_back[e % RING], 16)

        sp.wait_ge(o_out, 128 * HEADS + 16)
        sp.wait_ge(silu_out, 128 * HEADS + 16)
        for half in range(2):
            first = LAST_0 + half * HALF_BLOCKS
            at = half * HALF
            with sp.Fori(0, YB_BLOCKS // RING - 1) as i:
                for j in range(RING):
                    load_block(4 * i, first + j)
                    sp.wait_ge(o_ready, 4 * i + (half * YB_BLOCKS + j + 1))
                    load_o(half, i, j + RING)
            if half:
                sp.wait_ge(merged_ready, half * KT)
            else:
                sp.wait_ge(gate_b_out, 16 * KT)
            sp.dma_start(gate_b_in[:, :, :], gate_b_d[:, :, at:at + HALF].rearrange("k p t -> p k t"))\
                .then_inc(gates_back, 16)
            sp.dma_start(mixed_in[:, :, :], mixed_a_d[:, :, at:at + HALF].rearrange("k p t -> p k t"))\
                .then_inc(gates_back, 16)
            if half == 0:
                sp.dma_start(final_sb[:, :], final_g).then_inc(final_in, 16)
            for j in range(RING):
                load_block(0, first + YB_BLOCKS - RING + j)
            if half:
                sp.wait_ge(first_out, 16 * OUT_TILES)
            sp.dma_start(result[:, :, :], x_rows[half * OUT_TILES:(half + 1) * OUT_TILES].rearrange("t p n -> p t n"))\
                .then_inc(result_in, 16)
            for k in range(OUT_BLOCKS):
                if first + YB_BLOCKS + k + RAW + 2 < STREAM:
                    load_block(0, first + YB_BLOCKS + k)
                if half == 0 and k < RING:
                    sp.wait_ge(o_ready, YB_BLOCKS - RING + k + 1)
                    load_o(1, 0, k)
        for t in range(OUT_TILES - 1):
            sp.wait_ge(result_ready, OUT_TILES + t + 1)
            sp.dma_start(out[OUT_TILES + t], result[:, t, :]).then_inc(result_out, 16)
        for c in range(2):
            sp.wait_ge(result_ready, 2 * OUT_TILES + c)
            w = slice(c * BANK, (c + 1) * BANK)
            sp.dma_start(out[TT - 1, :, w], result[:, OUT_TILES - 1, w]).then_inc(result_out, 16)
        sp.wait_ge(result_out, (OUT_TILES + 1) * 16)

    @block.gpsimd
    def _(pool):
        pool.memset(ones[:, :], 1.0).then_inc(pool_consts, 1)
        pool.memset(minus_half, -0.5).then_inc(pool_consts, 1)
        pool.memset(eps, EPS).then_inc(pool_consts, 1)
        pool.wait_ge(pool_consts, 3)
        pool.wait_ge(var_ready, 1)
        nc.gpsimd.tensor_tensor(rms_scale, rms_var, minus_half, ALU.pow).then_inc(rms_ready, 1)
        for k in range(1, KT, 2):
            pool.wait_ge(h_hi_ready, k + 1)
            nc.gpsimd.tensor_tensor(h_lo[:, k, :], x_raw[:, k % X_RING, :], h_hi[:, k, :].bitcast(F32), ALU.subtract)\
                .then_inc(h_ready[1], 1)

        def o_factor(h, n):
            v = rms_var[:, n % 2:n % 2 + 1]
            r = rms_scale[:, n % 2:n % 2 + 1]
            pool.wait_ge(o_square_ready, TT * h + (n + 1))
            nc.gpsimd.tensor_tensor(v, square_sum[:, n % 2:n % 2 + 1], eps, ALU.add)\
                .then_inc(o_var_ready, 1)
            pool.wait_ge(o_var_ready, 2 * TT * h + (2 * n + 1))
            nc.gpsimd.tensor_tensor(r, v, minus_half[:, 0:1], ALU.pow).then_inc(o_var_ready, 1)
            pool.wait_ge(o_var_ready, 2 * TT * h + (2 * n + 2))
            nc.gpsimd.tensor_tensor(r, r, xi, ALU.mult).then_inc(o_scale_ready, 1)

        with pool.Fori(0, HEADS) as h:
            pool.wait_ge(table_in, 16 * h + 16)
            for n in range(TT):
                o_factor(h, n)

        pool.wait_ge(pair_read[2], ret_read(2, HEADS - 1, TT // 2 - 1))
        pool.wait_ge(o_out, 128 + 16)
        pool.wait_ge(silu_out, 128 + 16)
        for e in range(RING):
            pool.dma_start(o_raw[:, e, :], o_d[0, e]).then_inc(first_back[e], 16)
            pool.dma_start(silu_raw[:, e, :], silu_d[e, :, 0:HALF]).then_inc(first_back[e], 16)

        for t in range(2 * OUT_TILES):
            if t == OUT_TILES:
                pool.wait_ge(result_ready, t)
                pool.dma_start(out[t - 1], result[:, t - 1, :]).then_inc(first_out, 16)
            v, r = rms_var[:, t % 2:t % 2 + 1], rms_scale[:, t % 2:t % 2 + 1]
            total = square_sum[:, t % 2:t % 2 + 1]
            pool.wait_ge(last_square_ready, t + 1)
            if t == 2 * OUT_TILES - 1:
                pool.wait_ge(last_square_ready, t + 2)
                nc.gpsimd.tensor_tensor(total, square_sum[:, 2:3], square_sum[:, 3:4], ALU.add)\
                    .then_inc(last_total_ready, 1)
                pool.wait_ge(last_total_ready, 1)
            nc.gpsimd.tensor_scalar(v, total, 1.0 / D, EPS, ALU.mult, ALU.add)\
                .then_inc(last_var_ready, 1)
            pool.wait_ge(last_var_ready, t + 1)
            nc.gpsimd.tensor_tensor(r, v, minus_half[:, 0:1], ALU.pow).then_inc(last_scale_ready, 1)
            if 1 <= t < OUT_TILES:
                pool.wait_ge(result_ready, t)
                pool.dma_start(out[t - 1], result[:, t - 1, :]).then_inc(first_out, 16)

    @block.scalar
    def _(act):
        def split_hi(b, offset):
            n = offset
            act.wait_ge(raw_in[n % RAW], 8 * b + 16 * (n // RAW + 1))
            act.wait_ge(block_done, b + (n + 1))
            nc.scalar.activation(w_hi[:, n % RING, :], w_raw[:, n % RAW, :], ACT.Copy).then_inc(hi_ready, 1)

        act.wait_ge(pool_consts, 3)
        nc.scalar.activation(unused_col, eps[:, 0:1], ACT.Copy)

        act.wait_ge(consts_in, 16)

        def xg_high(k, tokens):
            return nc.scalar.activation(xg_hi[:, k, tokens], x_raw[:, k % X_RING, tokens], ACT.Copy, scale=g_col(k))

        def w_high(n, columns):
            return nc.scalar.activation(w_hi[:, n, columns], w_raw[:, n, columns], ACT.Copy)

        act.wait_ge(x_first_in, 16)
        xg_high(0, slice(0, HALF)).then_inc(first_hi, 1)
        act.wait_ge(w_first_in[0], 16)
        w_high(0, FIRST).then_inc(first_hi, 1)
        act.wait_ge(x_in[0], 16)
        xg_high(0, slice(HALF, T)).then_inc(xg_hi_ready, 1)
        act.wait_ge(w_first_in[1], 16)
        w_high(1, FIRST).then_inc(first_hi, 1)
        for k in range(1, KT):
            act.wait_ge(x_in[k % X_RING], 16 * (k // X_RING + 1))
            xg_high(k, slice(0, T)).then_inc(xg_hi_ready, 1)
            if k == 2:
                for n in range(2):
                    act.wait_ge(raw_in[n], 16)
                    w_high(n, SECOND).then_inc(hi_ready, 1)
        for t in range(TT):
            act.wait_ge(rows_in[t], 16)
            nc.scalar.activation(rows_raw[:, t, :], rows_raw[:, t, :], ACT.Square,
                                 accum_out=square_sum[:, t:t + 1]).then_inc(squares_ready, 1)
            if t == TT // 2 - 1:
                split_hi(0, 2)
        split_hi(0, 3)

        def scaled_gate(j):
            act.wait_ge(pair_read[j], READ_GB + 1 + (j == 3))
            nc.scalar.activation(gate_b[:, j, :], gate_b[:, j, :], ACT.Sigmoid).then_inc(gate_b_ready, 1)

        for k in range(KT):
            if k == 2:
                split_hi(0, 4)
                scaled_gate(0)
            act.wait_ge(h_scaled, k + 1)
            nc.scalar.activation(h_hi[:, k, :], x_raw[:, k % X_RING, :], ACT.Copy).then_inc(h_hi_ready, 1)
        split_hi(0, 5)
        for j in range(1, 4):
            scaled_gate(j)
        for j in range(GB_BLOCKS - 4):
            split_hi(0, 4 + j + 2)
            act.wait_ge(block_done, RING + 4 + j + 1)
            act.wait_ge(gate_b_out, 64)
            nc.scalar.activation(gate_b[:, j, :], pair(j), ACT.Sigmoid).then_inc(pair_read[j], 1)

        act.wait_ge(gate_b_out, 16 * GB_BLOCKS)
        with act.Fori(0, KT) as c:
            split_hi(4 * c, CONV_0 + 2)
            act.wait_ge(block_done, 4 * c + (RING + CONV_0 + 1))
            act.wait_ge(conv_step, CONV_STEPS * c + 3)
            nc.scalar.activation(u_pad[:, CONV - 1:], pair(0), ACT.Copy).then_inc(pair_read[0], 1)
            split_hi(4 * c, CONV_0 + 3)
            split_hi(4 * c, CONV_0 + 4)
            act.wait_ge(block_done, 4 * c + (RING + CONV_0 + 3))
            act.wait_ge(conv_step, CONV_STEPS * c + 4)
            nc.scalar.activation(gate_zb[:, :], pair(2), ACT.Sigmoid).then_inc(sig_c_ready, 1)
            split_hi(4 * c, CONV_0 + 5)

        act.wait_ge(y_ready, KT)
        with act.Fori(0, KT // 2) as i:
            for j in (0, 2):
                split_hi(4 * i, MIX_0 + j + 2)
                act.wait_ge(block_done, 4 * i + (RING + MIX_0 + j + 1))
                act.wait_ge(pair_read[j + 1], i + READ_MIX)
                nc.scalar.activation(sig_a[:, j // 2, :], pair(j), ACT.Sigmoid).then_inc(pair_read[j], 1)
                split_hi(4 * i, MIX_0 + j + 3)

        def score_parts(h, n):
            act.wait_ge(score_made, TT * h + (n + 1))
            if n >= 2:
                act.wait_ge(bank_full[4 + n % 2], full_head(4, h, 1 + (n - 2) // 2))
            nc.scalar.activation(score_hi[:, n % 2, :], scored[:, :], ACT.Copy).then_inc(score_hi_ready, 1)
            if n < TT - 1:
                nc.scalar.activation(key_hi[:, n % 2, :], psum[:, n % 2, P:P + QK], ACT.Copy)\
                    .then_inc(score_hi_ready, 1)

        def state_parts(h, n):
            act.wait_ge(pair_read[1], ret_read(1, h, n))
            if n >= 2:
                act.wait_ge(bank_full[4 + (n - 1) % 2], full_head(4, h, 1 + (n - 1) // 2))
            nc.scalar.activation(state_hi[:, n % 2, :], state[:, :], ACT.Copy).then_inc(state_hi_ready, 1)

        def o_back_copy(h, n):
            act.wait_ge(bank_full[7], full_head(7, h, 1 + n))
            act.wait_ge(o_out, 128 * h + 16 * (n + 1))
            nc.scalar.activation(o_t[:, :, :].rearrange("p e c -> p (e c)"), psum[:, 7, :], ACT.Copy)\
                .then_inc(pair_read[3], 1)

        act.wait_ge(block_done, RING + HEAD_0)
        for n in range(TT):
            last = nc.scalar.activation(q_hi[:, n, 1, :], ident[:, :], ACT.Copy)
        last.then_inc(beside_q, 1)
        with act.Fori(0, HEADS) as h:
            for j in range(4):
                split_hi(HEAD_BLOCKS * h, HEAD_0 + j + 2)
                if j % 2:
                    for d in range(DQ):
                        dst = q_hi[:, :, 2 * d, :] if j == 1 else by_chunk(k_hi[:, d, :])
                        act.wait_ge(turn_step, 2 * TURN_STEPS * h + (TURN_STEPS * (1 + j // 2) + 3 + d))
                        nc.scalar.activation(dst, by_chunk(turn[:, 2 * d, :]), ACT.Copy).then_inc(turn_hi_ready, 1)
            for s in range(4):
                split_hi(HEAD_BLOCKS * h, HEAD_0 + 4 + s + 2)
            act.wait_ge(turn_step, 2 * TURN_STEPS * h + 3 * TURN_STEPS)
            for t in range(TT):
                if t < BANKS - 1:
                    act.wait_ge(bank_full[t], full_head(t, h, 0))
                else:
                    act.wait_ge(block_done, HEAD_BLOCKS * h + (RING + HEAD_0 + SILU_0))
                nc.scalar.activation(v_hi[:, t, :], psum[:, t, :], ACT.Copy).then_inc(v_hi_ready, 1)
            score_parts(h, 0)
            score_parts(h, 1)
            act.wait_ge(table_in, 16 * h + 16)

            def silu_sigmoid(m):
                if m % 2 == 0:
                    split_hi(HEAD_BLOCKS * h, HEAD_0 + SILU_0 + m // 2 + 2)
                    act.wait_ge(bank_full[6], full_head(6, h, m // 2 + 1))
                else:
                    act.wait_ge(block_done, HEAD_BLOCKS * h + (RING + HEAD_0 + SILU_0 + m // 2 + 1))
                act.wait_ge(silu_out, 128 * h + (16 * m + 16))
                nc.scalar.activation(silu_z[:, :], psum[:, 6, :], ACT.Sigmoid).then_inc(sig_z_ready, 1)

            def o_squares(n):
                act.wait_ge(bank_full[4 + n % 2], full_head(4, h, 1 + n // 2))
                if n:
                    act.wait_ge(o_square_ready, TT * h + n)
                nc.scalar.activation(unused[:, :], psum[:, 4 + n % 2, :], ACT.Square, scale=xi_mean,
                                     accum_out=square_sum[:, n % 2:n % 2 + 1]).then_inc(o_square_ready, 1)

            def o_scaled(n):
                act.wait_ge(o_scale_ready, TT * h + (n + 1))
                nc.scalar.activation(o_rows[:, :], psum[:, 4 + n % 2, :], ACT.Copy,
                                     scale=rms_scale[:, n % 2:n % 2 + 1]).then_inc(pair_read[2], 1)

            silu_sigmoid(0)
            state_parts(h, 0)
            for n in range(TT):
                if n + 2 < TT:
                    score_parts(h, n + 2)
                o_squares(n)
                if n + 1 < TT - 1:
                    state_parts(h, n + 1)
                if n in SILU_AFTER:
                    silu_sigmoid(SILU_AFTER[n])
                if n:
                    o_back_copy(h, n - 1)
                o_scaled(n)
            silu_sigmoid(SILU_PARTS - 1)
            o_back_copy(h, TT - 1)

        def split_o_hi(i, e):
            act.wait_ge(o_gated, 4 * i + (e + 1))
            if e >= RING:
                half, tile = divmod(e - RING, YB_BLOCKS)
                act.wait_ge(block_done, 4 * i + (RING + LAST_0 + half * HALF_BLOCKS + tile + 1))
            nc.scalar.activation(o_hi[:, e % RING, :], o_raw[:, e % RING, :], ACT.Copy).then_inc(o_hi_ready, 1)

        split_hi(0, LAST_GATE + 2)
        split_o_hi(0, 0)
        split_o_hi(0, 1)
        act.wait_ge(block_done, RING + LAST_GATE + 1)
        act.wait_ge(state_ready, (TT - 1) * HEADS)
        nc.scalar.activation(last_gate[:, :], pair(2), ACT.Sigmoid).then_inc(pair_read[2], 1)

        for half in range(2):
            first, e0 = LAST_0 + half * HALF_BLOCKS, half * YB_BLOCKS
            for j in range(2):
                split_hi(0, first + j + 2)
                split_o_hi(0, e0 + j + 2)
            with act.Fori(0, YB_BLOCKS // RING - 1) as i:
                for j in range(2, 2 + RING):
                    split_hi(4 * i, first + j + 2)
                    split_o_hi(i, e0 + j + 2)
            for j in range(YB_BLOCKS - 2, YB_BLOCKS):
                split_hi(0, first + j + 2)
            for k in range(KT):
                act.wait_ge(merged_ready, half * KT + k + 1)
                if half and k == 0:
                    act.wait_ge(block_done, RING + LAST_0 + HALF_BLOCKS)
                nc.scalar.activation(m_hi[:, k, :], merged[:, k, :], ACT.Copy).then_inc(m_hi_ready, 1)
                if first + YB_BLOCKS + k + 2 < STREAM:
                    split_hi(0, first + YB_BLOCKS + k + 2)
            if half == 0:
                split_o_hi(0, YB_BLOCKS)
                split_o_hi(0, YB_BLOCKS + 1)
            for t in range(OUT_TILES - half):
                act.wait_ge(pair_read[t], last_read(t, half, 3))
                if half or t:
                    act.wait_ge(last_square_ready, half * OUT_TILES + t)
                nc.scalar.activation(unused_last[:, :], result[:, t, :], ACT.Square,
                                     accum_out=square_sum[:, t % 2:t % 2 + 1]).then_inc(last_square_ready, 1)
        t = OUT_TILES - 1
        for c in range(2):
            act.wait_ge(pair_read[t], last_read(t, 1, 3 + c))
            act.wait_ge(last_square_ready, 2 * OUT_TILES - 1 + c)
            w = slice(c * BANK, (c + 1) * BANK)
            nc.scalar.activation(unused_last[:, w], result[:, t, w], ACT.Square,
                                 accum_out=square_sum[:, 2 + c:3 + c]).then_inc(last_square_ready, 1)

    @block.vector
    def _(dve):
        def split_lo(b, offset):
            n = offset
            dve.wait_ge(hi_ready, b + (n + 1))
            nc.vector.tensor_tensor(w_lo[:, n % RING, :], w_raw[:, n % RAW, :], w_hi[:, n % RING, :].bitcast(F32),
                                    ALU.subtract).then_inc(parts_ready, 1)

        for j in range(BANKS // 2):
            dve.sem_inc(pair_read[j], 1)
        dve.sem_inc(conv_step, CONV_STEPS)
        dve.sem_inc(turn_step, TURN_STEPS)
        dve.sem_inc(silu_read, SILU_PARTS)

        dve.wait_ge(consts_in, 16)

        def xg_low(k, tokens):
            return nc.vector.scalar_tensor_tensor(xg_lo[:, k, tokens], x_raw[:, k % X_RING, tokens], g_col(k),
                                                  xg_hi[:, k, tokens].bitcast(F32), ALU.mult, ALU.subtract)

        def w_low(n, columns):
            return nc.vector.tensor_tensor(w_lo[:, n, columns], w_raw[:, n, columns],
                                           w_hi[:, n, columns].bitcast(F32), ALU.subtract)

        dve.wait_ge(first_hi, 1)
        xg_low(0, slice(0, HALF)).then_inc(first_ready, 1)
        dve.wait_ge(first_hi, 2)
        w_low(0, FIRST).then_inc(first_ready, 1)
        dve.wait_ge(xg_hi_ready, 1)
        xg_low(0, slice(HALF, T)).then_inc(xg_ready, 1)
        dve.wait_ge(first_hi, 3)
        w_low(1, FIRST).then_inc(first_ready, 1)
        for k in range(1, KT):
            dve.wait_ge(xg_hi_ready, k + 1)
            xg_low(k, slice(0, T)).then_inc(xg_ready, 1)
            if k == 2:
                for n in range(2):
                    dve.wait_ge(hi_ready, n + 1)
                    w_low(n, SECOND).then_inc(parts_ready, 1)
        split_lo(0, 2)
        dve.wait_ge(squares_ready, TT)
        nc.vector.tensor_scalar(rms_var, square_sum, 1.0 / D, EPS, ALU.mult, ALU.add).then_inc(var_ready, 1)
        split_lo(0, 3)
        dve.wait_ge(rms_ready, 1)
        dve.wait_ge(ident_in, 16)
        for t in range(TT):
            nc.vector.tensor_scalar(diagonal[:, t, :], ident[:, :], rms_scale[:, t:t + 1], None, ALU.mult)\
                .then_inc(diag_ready, 1)
        dve.wait_ge(factors_full, 2)
        nc.vector.tensor_copy(factors[:, :], pair(3)).then_inc(pair_read[3], 1)

        def scaled_gate(j):
            dve.wait_ge(block_done, RING + j + 1)
            nc.vector.tensor_tensor(gate_b[:, j, :], pair(j), factors[:, :], ALU.mult).then_inc(pair_read[j], 1)

        def h_low(k):
            dve.wait_ge(h_hi_ready, k + 1)
            nc.vector.tensor_tensor(h_lo[:, k, :], x_raw[:, k % X_RING, :], h_hi[:, k, :].bitcast(F32), ALU.subtract)\
                .then_inc(h_ready[0], 1)

        dve.wait_ge(pair_read[3], READ_GB + 1)
        for k in range(KT):
            dve.wait_ge(x_in[k % X_RING], 32 + 16 * (k // X_RING + 1))
            nc.vector.scalar_tensor_tensor(x_raw[:, k % X_RING, :], x_raw[:, k % X_RING, :], g_col(k), factors[:, :],
                                           ALU.mult, ALU.mult).then_inc(h_scaled, 1)
            if k == 1:
                scaled_gate(0)
                split_lo(0, 4)
            if k % 2:
                h_low(k - 1)
        split_lo(0, 5)
        for j in range(1, 4):
            scaled_gate(j)
        for j in range(GB_BLOCKS - 4):
            split_lo(0, 4 + j + 2)

        dve.wait_ge(gate_b_out, 16 * GB_BLOCKS)
        nc.vector.memset(u_pad[:, 0:CONV - 1], 0.0)
        with dve.Fori(0, KT) as c:
            def step(n):
                return CONV_STEPS * c + (CONV_STEPS + n)

            def conv_col(n):
                return cols[:, bass.ds(c + (1 + n) * KT, 1)]

            split_lo(4 * c, CONV_0 + 2)
            split_lo(4 * c, CONV_0 + 3)
            dve.wait_ge(pair_read[0], c + (READ_CONV + 1))
            dve.wait_ge(block_done, 4 * c + (RING + CONV_0 + 2))
            nc.vector.tensor_tensor(u_pad[:, CONV - 1:], pair(1), u_pad[:, CONV - 1:], ALU.mult)\
                .then_inc(pair_read[1], 1)
            dve.wait_ge(pair_read[1], c + (READ_CONV + 1))
            nc.vector.tensor_scalar(taps[:, :], u_pad[:, 0:T], conv_col(0), conv_col(CONV), ALU.mult, ALU.add)\
                .then_inc(conv_step, 1)
            for n in range(1, CONV):
                dve.wait_ge(conv_step, step(n))
                nc.vector.scalar_tensor_tensor(taps[:, :], u_pad[:, n:n + T], conv_col(n), taps[:, :],
                                               ALU.mult, ALU.add).then_inc(conv_step, 1)
            split_lo(4 * c, CONV_0 + 4)
            dve.wait_ge(sig_c_ready, c + 1)
            nc.vector.tensor_tensor(gate_zb[:, :], pair(2), gate_zb[:, :], ALU.mult)\
                .then_inc(pair_read[2], 1)
            split_lo(4 * c, CONV_0 + 5)
            dve.wait_ge(block_done, 4 * c + (RING + CONV_0 + 4))
            dve.wait_ge(pair_read[2], c + (READ_CONV + 1))
            nc.vector.tensor_tensor(gate_zb[:, :], pair(3), gate_zb[:, :], ALU.mult)\
                .then_inc(pair_read[3], 1)
            dve.wait_ge(pair_read[3], c + (READ_CONV + 1))
            dve.wait_ge(conv_step, step(3))
            nc.vector.tensor_tensor(taps[:, :], gate_zb[:, :], taps[:, :], ALU.mult).then_inc(conv_step, 1)
            dve.wait_ge(conv_step, step(4))
            nc.vector.tensor_scalar(y_hi[:, c, :], taps[:, :], 1.0, None, ALU.mult).then_inc(conv_step, 1)
            dve.wait_ge(conv_step, step(5))
            nc.vector.tensor_tensor(y_lo[:, c, :], taps[:, :], y_hi[:, c, :].bitcast(F32), ALU.subtract)\
                .then_inc(y_ready, 1)

        with dve.Fori(0, KT // 2) as i:
            for j in (1, 3):
                split_lo(4 * i, MIX_0 + j + 1)
                split_lo(4 * i, MIX_0 + j + 2)
                dve.wait_ge(block_done, 4 * i + (RING + MIX_0 + j + 1))
                dve.wait_ge(pair_read[j - 1], i + (READ_MIX + 1))
                dve.wait_ge(mixed_out, 32 * i + 32)
                nc.vector.tensor_tensor(mixed_a[:, j // 2, :], pair(j), sig_a[:, j // 2, :], ALU.mult)\
                    .then_inc(pair_read[j], 1)

        def rotate(h, j):
            lo = [by_chunk((q_lo, k_lo)[j][:, d, :]) for d in range(DQ)]
            hi = [by_chunk(k_hi[:, d, :]) if j else q_hi[:, :, 2 * d, :] for d in range(DQ)]
            cos, sin = rope_sb[:, 0, :], rope_sb[:, 1, :]
            one, two = pair(2 * j), pair(2 * j + 1)
            at = 2 * TURN_STEPS * h + TURN_STEPS * (1 + j)
            dve.wait_ge(block_done, HEAD_BLOCKS * h + (RING + HEAD_0 + 2 * j + 2))
            dve.wait_ge(turn_step, at)
            nc.vector.tensor_tensor(turn[:, 0, :], one, cos, ALU.mult).then_inc(turn_step, 1)
            nc.vector.tensor_tensor(turn[:, 1, :], two, sin, ALU.mult).then_inc(turn_step, 1)
            nc.vector.tensor_tensor(turn[:, 2, :], one, sin, ALU.mult).then_inc(pair_read[2 * j], 1)
            nc.vector.tensor_tensor(turn[:, 3, :], two, cos, ALU.mult).then_inc(pair_read[2 * j + 1], 1)
            dve.wait_ge(turn_step, at + 2)
            nc.vector.tensor_tensor(turn[:, 0, :], turn[:, 0, :], turn[:, 1, :], ALU.subtract).then_inc(turn_step, 1)
            for n in (2 * j, 2 * j + 1):
                dve.wait_ge(pair_read[n], head_read(n, h, 1))
            nc.vector.tensor_tensor(turn[:, 2, :], turn[:, 2, :], turn[:, 3, :], ALU.add).then_inc(turn_step, 1)
            for d in range(DQ):
                dve.wait_ge(turn_hi_ready, 4 * h + (2 * j + d + 1))
                nc.vector.tensor_tensor(lo[d], by_chunk(turn[:, 2 * d, :]), hi[d].bitcast(F32), ALU.subtract)\
                    .then_inc(turn_step, 1)

        def score(h, n):
            at = psum[:, n % 2, :]
            dve.wait_ge(bank_full[n % 2], full_head(0, h, 1 + n // 2))
            dve.wait_ge(pair_read[0], head_read(0, h, 3 + n))
            if n < TT - 1:
                nc.vector.tensor_tensor(scored[:, :], at[:, P + QK:], decay, ALU.mult)
                nc.vector.tensor_tensor(at[:, 0:P], at[:, 0:P], decay, ALU.mult).then_inc(score_decayed, 1)
                nc.vector.tensor_scalar(at[:, P:P + QK], at[:, P:P + QK], key_decay, None, ALU.mult)
                dve.wait_ge(score_decayed, (TT - 1) * h + (n + 1))
                nc.vector.tensor_tensor(scored[:, :], at[:, 0:P], scored[:, :], ALU.add).then_inc(score_made, 1)
            else:
                nc.vector.tensor_tensor(scored[:, :], at[:, 0:P], decay, ALU.mult).then_inc(score_made, 1)
            parts = 2 if n < TT - 1 else 1
            dve.wait_ge(score_hi_ready, (2 * TT - 1) * h + (2 * n + parts))
            if n < TT - 1:
                nc.vector.tensor_tensor(key_lo[:, n % 2, :], at[:, P:P + QK], key_hi[:, n % 2, :].bitcast(F32),
                                        ALU.subtract)
            nc.vector.tensor_tensor(score_lo[:, n % 2, :], scored[:, :], score_hi[:, n % 2, :].bitcast(F32),
                                    ALU.subtract).then_inc(pair_read[0], 1)

        def new_state(h, n):
            for b in (2, 3):
                dve.wait_ge(bank_full[b], full_head(b, h, 1 + n))
            if n == 0:
                made = nc.vector.tensor_copy(state[:, :], pair(1))
            else:
                dve.wait_ge(state_ready, (TT - 1) * h + n)
                made = nc.vector.scalar_tensor_tensor(state[:, :], state[:, :], chunk_decay, pair(1), ALU.mult, ALU.add)
            made.then_inc(pair_read[1], 1)

        def state_low(h, n):
            dve.wait_ge(state_hi_ready, (TT - 1) * h + (n + 1))
            nc.vector.tensor_tensor(state_lo[:, n % 2, :], state[:, :], state_hi[:, n % 2, :].bitcast(F32),
                                    ALU.subtract).then_inc(state_ready, 1)

        with dve.Fori(0, HEADS) as h:
            for j in range(4):
                split_lo(HEAD_BLOCKS * h, HEAD_0 + j + 2)
                if j % 2:
                    dve.wait_ge(rope_in, 16 * h + 16)
                    rotate(h, j // 2)
            for s in range(4):
                split_lo(HEAD_BLOCKS * h, HEAD_0 + 4 + s + 2)
            for t in range(TT):
                dve.wait_ge(v_hi_ready, TT * h + (t + 1))
                nc.vector.tensor_tensor(v_lo[:, t, :], psum[:, t, :], v_hi[:, t, :].bitcast(F32), ALU.subtract)\
                    .then_inc(pair_read[t // 2], 1)
            dve.wait_ge(table_in, 16 * h + 16)
            score(h, 0)
            score(h, 1)

            def silu_product(m):
                dve.wait_ge(sig_z_ready, SILU_PARTS * h + (m + 1))
                nc.vector.tensor_tensor(silu_z[:, :], psum[:, 6, :], silu_z[:, :], ALU.mult).then_inc(silu_read, 1)
                if m % 2 == 0:
                    split_lo(HEAD_BLOCKS * h, HEAD_0 + SILU_0 + m // 2 + 2)

            new_state(h, 0)
            silu_product(0)
            state_low(h, 0)
            for n in range(TT):
                if n + 2 < TT:
                    score(h, n + 2)
                if n + 1 < TT - 1:
                    new_state(h, n + 1)
                    state_low(h, n + 1)
                if n in SILU_AFTER:
                    silu_product(SILU_AFTER[n])
            silu_product(SILU_PARTS - 1)

        def split_o_lo(i, e):
            dve.wait_ge(o_hi_ready, 4 * i + (e + 1))
            nc.vector.tensor_tensor(o_lo[:, e % RING, :], o_raw[:, e % RING, :], o_hi[:, e % RING, :].bitcast(F32),
                                    ALU.subtract).then_inc(o_ready, 1)

        def gate_o(i, e):
            n = e % RING
            if e < RING:
                dve.wait_ge(first_back[n], 32)
            else:
                dve.wait_ge(o_back[n], 16 * i + 16 * (e // RING))
                dve.wait_ge(silu_back[n], 16 * i + 16 * (e // RING))
            nc.vector.tensor_tensor(o_raw[:, n, :], o_raw[:, n, :], silu_raw[:, n, :], ALU.mult).then_inc(o_gated, 1)

        gate_o(0, 0)
        gate_o(0, 1)
        split_o_lo(0, 0)
        split_o_lo(0, 1)
        split_lo(0, LAST_GATE + 2)
        for half in range(2):
            first, e0 = LAST_0 + half * HALF_BLOCKS, half * YB_BLOCKS
            for j in range(2):
                gate_o(0, e0 + j + 2)
                split_lo(0, first + j + 2)
                split_o_lo(0, e0 + j + 2)
            with dve.Fori(0, YB_BLOCKS // RING - 1) as i:
                for j in range(2, 2 + RING):
                    gate_o(i, e0 + j + 2)
                    split_lo(4 * i, first + j + 2)
                    split_o_lo(i, e0 + j + 2)
            for j in range(YB_BLOCKS - 2, YB_BLOCKS):
                split_lo(0, first + j + 2)
            dve.wait_ge(gates_back, 32 * (half + 1))
            n0 = half * KT

            def gated(k):
                if k < BANKS - 1:
                    dve.wait_ge(bank_full[k], full_last(k, half, 0))
                else:
                    dve.wait_ge(block_done, RING + first + YB_BLOCKS)
                nc.vector.tensor_tensor(merged[:, k, :], psum[:, k, :], gate_b_in[:, k, :], ALU.mult)\
                    .then_inc(pair_read[k // 2], 1)

            def add_mixed(k):
                dve.wait_ge(pair_read[k // 2], last_read(k // 2, half, k % 2 + 1))
                nc.vector.tensor_tensor(merged[:, k, :], merged[:, k, :], mixed_in[:, k, :], ALU.add)\
                    .then_inc(merged_ready, 1)

            def merged_lo(k):
                dve.wait_ge(m_hi_ready, n0 + k + 1)
                nc.vector.tensor_tensor(m_lo[:, k, :], merged[:, k, :], m_hi[:, k, :].bitcast(F32), ALU.subtract)\
                    .then_inc(m_ready, 1)

            gated(0)
            gated(1)
            add_mixed(0)
            gated(2)
            merged_lo(0)
            for k in range(3, KT):
                gated(k)
            for k in range(1, KT):
                add_mixed(k)
                if first + YB_BLOCKS + k + 1 < STREAM:
                    split_lo(0, first + YB_BLOCKS + k + 1)
                merged_lo(k)
            if half == 0:
                split_lo(0, first + YB_BLOCKS + OUT_BLOCKS + 1)
                gate_o(0, YB_BLOCKS)
                gate_o(0, YB_BLOCKS + 1)
                split_o_lo(0, YB_BLOCKS)
                split_o_lo(0, YB_BLOCKS + 1)
            dve.wait_ge(result_in, 16 * (half + 1))
            dve.wait_ge(final_in, 16)

            def add_x(t):
                dve.wait_ge(bank_full[2 * t], full_last(2 * t, half, 1))
                if t < OUT_TILES - 1:
                    dve.wait_ge(bank_full[2 * t + 1], full_last(2 * t + 1, half, 1))
                else:
                    dve.wait_ge(block_done, RING + first + HALF_BLOCKS)
                nc.vector.tensor_tensor(result[:, t, :], pair(t), result[:, t, :], ALU.add)\
                    .then_inc(pair_read[t], 1)

            def normed(t, columns=slice(0, D)):
                dve.wait_ge(last_scale_ready, half * OUT_TILES + t + 1)
                nc.vector.scalar_tensor_tensor(result[:, t, columns], result[:, t, columns],
                                               rms_scale[:, t % 2:t % 2 + 1], final_sb[:, columns],
                                               ALU.mult, ALU.mult).then_inc(result_ready, 1)

            add_x(0)
            for t in range(1, OUT_TILES - half):
                add_x(t)
                normed(t - 1)
            if half == 0:
                normed(OUT_TILES - 1)
        t = OUT_TILES - 1
        for c in range(2):
            if c == 0:
                dve.wait_ge(bank_full[2 * t], full_last(2 * t, 1, 1))
            else:
                normed(t - 1)
                dve.wait_ge(block_done, RING + STREAM)
            w = slice(c * BANK, (c + 1) * BANK)
            nc.vector.tensor_tensor(result[:, t, w], psum[:, 2 * t + c, :], result[:, t, w], ALU.add)\
                .then_inc(pair_read[t], 1)
        for c in range(2):
            normed(t, slice(c * BANK, (c + 1) * BANK))

    @block.tensor
    def _(pe):
        def product(dst, left, right, start, stop, l=slice(None), r=slice(None)):
            (l_hi, l_lo), (r_hi, r_lo) = left, right
            nc.tensor.matmul(dst, l_hi, r_hi, start=start, stop=False)
            nc.tensor.matmul(dst, l_hi, r_lo, start=False, stop=False)
            return nc.tensor.matmul(dst, l_lo, r_hi, start=False, stop=stop)

        def channel_block(b, n, j, read, hi, lo, arrived=None, before_last=None):
            pe.wait_ge(parts_ready, b + (n + 1))
            pe.wait_ge(pair_read[j], read)
            slot = n % RING
            for k in range(KT):
                if arrived:
                    pe.wait_ge(*arrived(k))
                if k == KT - 2 and before_last:
                    before_last()
                w = slice(k * P, (k + 1) * P)
                for part in range(2):
                    t = slice(part * BANK, (part + 1) * BANK)
                    last = product(psum[:, 2 * j + part, :], (w_hi[:, slot, w], w_lo[:, slot, w]),
                                   (hi[:, k, t], lo[:, k, t]), k == 0, k == KT - 1)
            last.then_inc(block_done, 1)

        def row_blocks(b, n, read):
            for s in range(4):
                pe.wait_ge(parts_ready, b + (n + s + 1))
                slot = (n + s) % RING
                groups = 2 if s == 0 else 1
                for kk, t in ((kk, t) for g in range(groups) for kk in range(2)
                              for t in range(g * TT // groups, (g + 1) * TT // groups)):
                    k = 2 * s + kk
                    if k == 0 and t % 2 == 0:
                        pe.wait_ge(pair_read[t // 2], read(t // 2))
                    rows, c = slice(t * P, (t + 1) * P), slice(kk * V, (kk + 1) * V)
                    last = product(psum[:, t, :], (h_hi[:, k, rows], h_lo[:, k, rows]),
                                   (w_hi[:, slot, c], w_lo[:, slot, c]), k == 0, k == KT - 1)
                    if k == KT - 1 and t < BANKS - 1:
                        last.then_inc(bank_full[t], 1)
                last.then_inc(block_done, 1)

        pe.sem_inc(block_done, RING)

        pe.wait_ge(pool_consts, 1)
        for n in range(WARM_UP):
            nc.tensor.matmul(psum[:, 7, 0:P], ones[:, :], ones[:, :], start=True, stop=True)

        def spread_factors():
            pe.wait_ge(pool_consts, 3)
            for part in range(2):
                pe.wait_ge(diag_ready, (part + 1) * TT // 2)
                nc.tensor.matmul(psum[:, 6 + part, :], ones[:, :],
                                 diagonal[:, part * TT // 2:(part + 1) * TT // 2, :].rearrange("p t n -> p (t n)"),
                                 start=True, stop=True).then_inc(factors_full, 1)

        for j in range(2):
            pe.wait_ge(pair_read[j], READ_GB)
        for k in range(KT):
            w = slice(k * P, (k + 1) * P)
            for j in range(2):
                if k == 0:
                    pe.wait_ge(first_ready, j + 2)
                if k == KT // 2:
                    pe.wait_ge(parts_ready, j + 1)
                for part in range(2):
                    if k or part:
                        pe.wait_ge(xg_ready, k + 1)
                    t = slice(part * BANK, (part + 1) * BANK)
                    last = product(psum[:, 2 * j + part, :], (w_hi[:, j, w], w_lo[:, j, w]),
                                   (xg_hi[:, k, t], xg_lo[:, k, t]), k == 0, k == KT - 1)
                if k == KT - 1:
                    last.then_inc(block_done, 1)
        channel_block(0, 2, 2, READ_GB, xg_hi, xg_lo, before_last=spread_factors)
        channel_block(0, 3, 3, READ_GB + 1, xg_hi, xg_lo)
        for j in range(GB_BLOCKS - 4):
            channel_block(0, 4 + j, j, READ_GB + 1, h_hi, h_lo,
                          (lambda k: (h_ready[k % 2], k // 2 + 1)) if j == 0 else None)

        with pe.Fori(0, KT) as c:
            for j in range(4):
                channel_block(4 * c, CONV_0 + j, j, c + READ_CONV, h_hi, h_lo)

        with pe.Fori(0, KT // 2) as i:
            for j in range(4):
                if j == 1:
                    pe.wait_ge(y_ready, KT)
                hi, lo = (y_hi, y_lo) if j % 2 else (h_hi, h_lo)
                channel_block(4 * i, MIX_0 + j, j, i + READ_MIX, hi, lo)

        def chunk(n):
            return slice(n * P, (n + 1) * P)

        def scores(h, n):
            bank = n % 2
            pe.wait_ge(pair_read[0], head_read(0, h, 3 + max(n - 1, 0)))
            for d in range(DQ):
                keys, q_high = (k_hi[:, d, chunk(n)], k_lo[:, d, chunk(n)]), q_hi[:, n, 2 * d, :]
                if n == TT - 1:
                    last = product(psum[:, bank, 0:P], keys, (q_high, q_lo[:, d, chunk(n)]), d == 0, d == DQ - 1)
                else:
                    scores_at = psum[:, bank, 3 * d * P:(3 * d + 1) * P]
                    both = psum[:, bank, 2 * d * P:2 * (d + 1) * P]
                    q_and_identity = q_hi[:, n, d:d + 2, :].rearrange("p b c -> p (b c)")
                    nc.tensor.matmul(both, keys[0], q_and_identity, start=True, stop=False)
                    nc.tensor.matmul(scores_at, keys[0], q_lo[:, d, chunk(n)], start=False, stop=False)
                    last = nc.tensor.matmul(both, keys[1], q_and_identity, start=False, stop=True)
            last.then_inc(bank_full[bank], 1)

        def update(h, n):
            pe.wait_ge(pair_read[0], ret_read(0, h, n))
            pe.wait_ge(pair_read[1], head_read(1, h, 3 + n))
            for d in range(DQ):
                c = slice(d * P, (d + 1) * P)
                product(psum[:, 2 + d, :], (key_hi[:, n % 2, c], key_lo[:, n % 2, c]),
                        (v_hi[:, n, :], v_lo[:, n, :]), True, True).then_inc(bank_full[2 + d], 1)

        def rows(h, n):
            bank = 4 + n % 2
            pe.wait_ge(pair_read[2], head_read(2, h, 3 + max(n - 1, 0)))
            pe.wait_ge(pair_read[0], ret_read(0, h, n))
            last = product(psum[:, bank, :], (score_hi[:, n % 2, :], score_lo[:, n % 2, :]),
                           (v_hi[:, n, :], v_lo[:, n, :]), True, n == 0)
            if n:
                pe.wait_ge(state_ready, (TT - 1) * h + n)
                for d in range(DQ):
                    c = slice(d * V, (d + 1) * V)
                    last = product(psum[:, bank, :], (q_hi[:, n, 2 * d, :], q_lo[:, d, chunk(n)]),
                                   (state_hi[:, (n - 1) % 2, c], state_lo[:, (n - 1) % 2, c]), False, d == DQ - 1)
            last.then_inc(bank_full[bank], 1)

        def transposed(h, n):
            bank = 7
            pe.wait_ge(pair_read[3], head_read(3, h, 3 + n))
            pe.wait_ge(pair_read[2], ret_read(2, h, n))
            for e in range(ET):
                last = nc.tensor.transpose(psum[:, bank, e * P:(e + 1) * P], o_rows[:, e * P:(e + 1) * P], ident[:, :])
            last.then_inc(bank_full[bank], 1)

        with pe.Fori(0, HEADS) as h:
            for j in range(4):
                if j == 3:
                    pe.wait_ge(silu_read, SILU_PARTS * h + SILU_PARTS)
                channel_block(HEAD_BLOCKS * h, HEAD_0 + j, j, head_read(j, h, 0), h_hi, h_lo)
            row_blocks(HEAD_BLOCKS * h, HEAD_0 + 4, lambda j: head_read(j, h, 1))
            pe.wait_ge(turn_step, 2 * TURN_STEPS * h + 3 * TURN_STEPS)
            pe.wait_ge(beside_q, 1)
            scores(h, 0)
            scores(h, 1)

            def silu_part(m):
                n, t = HEAD_0 + SILU_0 + m // 2, slice((m % 2) * HALF, (m % 2 + 1) * HALF)
                pe.wait_ge(parts_ready, HEAD_BLOCKS * h + (n + 1))
                if m:
                    pe.wait_ge(silu_read, SILU_PARTS * h + (SILU_PARTS + m))
                for k in range(KT):
                    w = slice(k * P, (k + 1) * P)
                    last = product(psum[:, 6, :], (w_hi[:, n % RING, w], w_lo[:, n % RING, w]),
                                   (h_hi[:, k, t], h_lo[:, k, t]), k == 0, k == KT - 1)
                last.then_inc(block_done if m % 2 else bank_full[6], 1)

            pe.wait_ge(pair_read[3], head_read(3, h, 2))
            silu_part(0)
            for j in range(BANKS // 2):
                pe.wait_ge(pair_read[j], head_read(j, h, 3))
            update(h, 0)
            for n in range(TT):
                if n + 2 < TT:
                    scores(h, n + 2)
                rows(h, n)
                if n + 1 < TT - 1:
                    update(h, n + 1)
                if n in SILU_AFTER:
                    silu_part(SILU_AFTER[n])
                if n:
                    transposed(h, n - 1)
            silu_part(SILU_PARTS - 1)
            transposed(h, TT - 1)

        channel_block(0, LAST_GATE, 2, head_read(2, HEADS, 0), h_hi, h_lo)

        def o_block(i, half, e, start, stop):
            n = LAST_0 + half * HALF_BLOCKS + e
            pe.wait_ge(parts_ready, 4 * i + (n + 1))
            pe.wait_ge(o_ready, 4 * i + (half * YB_BLOCKS + e + 1))
            slot = e % RING
            for d in range(KT):
                if start and d % 2 == 0:
                    pe.wait_ge(pair_read[d // 2], last_read(d // 2, half, 0))
                if start and d == 6:
                    pe.wait_ge(silu_read, SILU_PARTS * (HEADS + 1))
                w = slice(d * P, (d + 1) * P)
                last = product(psum[:, d, :], (w_hi[:, n % RING, w], w_lo[:, n % RING, w]),
                               (o_hi[:, slot, :], o_lo[:, slot, :]), start, stop)
                if stop and d < BANKS - 1:
                    last.then_inc(bank_full[d], 1)
            last.then_inc(block_done, 1)

        for half in range(2):
            for e in range(RING):
                o_block(0, half, e, e == 0, False)
            with pe.Fori(0, YB_BLOCKS // RING - 2) as i:
                for e in range(RING, 2 * RING):
                    o_block(i, half, e, False, False)
            for e in range(YB_BLOCKS - RING, YB_BLOCKS):
                o_block(0, half, e, False, e == YB_BLOCKS - 1)
            def out_product(k, t, c):
                n, bank = LAST_0 + half * HALF_BLOCKS + YB_BLOCKS + k, 2 * t + c
                if k == 0 and c == 0:
                    pe.wait_ge(pair_read[t], last_read(t, half, 2))
                w = slice(c * BANK, (c + 1) * BANK)
                last = product(psum[:, bank, :], (m_hi[:, k, chunk(t)], m_lo[:, k, chunk(t)]),
                               (w_hi[:, n % RING, w], w_lo[:, n % RING, w]), k == 0, k == OUT_BLOCKS - 1)
                if k == OUT_BLOCKS - 1 and bank < BANKS - 1:
                    last.then_inc(bank_full[bank], 1)
                return last

            by_tile = RING - 1 if half else 0
            for k in range(OUT_BLOCKS - by_tile):
                pe.wait_ge(parts_ready, LAST_0 + half * HALF_BLOCKS + YB_BLOCKS + k + 1)
                pe.wait_ge(m_ready, half * KT + k + 1)
                for t in range(OUT_TILES):
                    for c in range(2):
                        last = out_product(k, t, c)
                last.then_inc(block_done, 1)
            if by_tile:
                pe.wait_ge(parts_ready, STREAM)
                pe.wait_ge(m_ready, 2 * KT)
                for t in range(OUT_TILES):
                    for c in range(2):
                        for k in range(OUT_BLOCKS - by_tile, OUT_BLOCKS):
                            last = out_product(k, t, c)
                            if 2 * t + c == BANKS - 1:
                                last.then_inc(block_done, 1)

    held.close()


def weight_stream(w_in, w_a, w_b, w_o):
    def channels(w, c0):
        return w[:, c0:c0 + P].reshape(KT, P, P).transpose(1, 0, 2).reshape(P, BLOCK)

    def columns(w, c0):
        return [w[2 * s * P:(2 * s + 2) * P, c0:c0 + V].reshape(2, P, V).transpose(1, 0, 2).reshape(P, BLOCK)
                for s in range(4)]

    b0, c0, x0, z0, q0, k0 = (n * D for n in range(6))
    v0, zb0, ga0, gb0 = 6 * D, 8 * D, 10 * D, 11 * D
    gates = [channels(w_in, gb0 + d * P) for d in range(KT)]
    blocks = gates[:GB_BLOCKS]
    for c in range(KT):
        blocks += [channels(w_in, at + c * P) for at in (c0, x0, z0, b0)]
    for d in range(KT):
        blocks += [channels(w_in, ga0 + d * P), channels(w_a, d * P)]
    for h in range(HEADS):
        blocks += [channels(w_in, at + h * QK + d * P) for at in (q0, k0) for d in range(DQ)]
        blocks += columns(w_in, v0 + h * V)
        blocks += [channels(w_in, zb0 + h * V + e * P) for e in range(ET)]
    ends = [w_b[e * P:(e + 1) * P] for e in range(YB_BLOCKS)] + [w_o[k * P:(k + 1) * P] for k in range(OUT_BLOCKS)]
    return np.ascontiguousarray(np.stack(blocks + gates[GB_BLOCKS:] + ends + ends))


def kernel(x, norm_g, w_in, conv_w, conv_b, w_a_out, w_b_out, w_o, final_g):
    import concourse.bacc as bacc
    from concourse.bass_utils import run_bass_kernel_spmd

    x2 = np.asarray(x)[0]
    rope, table, identity = constants()
    per_tile = [np.asarray(norm_g)[0], *np.asarray(conv_w)[0], np.asarray(conv_b)[0]]
    arrays = {
        "x_t": np.ascontiguousarray(x2.T.reshape(KT, P, T)),
        "x_rows": np.ascontiguousarray(x2.reshape(TT, P, D)),
        "columns": np.ascontiguousarray(np.concatenate([a.reshape(KT, P).T for a in per_tile], axis=1)),
        "weights": weight_stream(*(np.asarray(w)[0] for w in (w_in, w_a_out, w_b_out, w_o))),
        "final_g": np.ascontiguousarray(np.broadcast_to(np.asarray(final_g), (P, D))),
        "rope": rope,
        "head_table": table,
        "identity": identity,
    }
    nc = bacc.Bacc("TRN2", target_bir_lowering=False, num_devices=1)
    aps = [nc.dram_tensor(name, a.shape, mybir.dt.from_np(a.dtype), kind="ExternalInput").ap()
           for name, a in arrays.items()]
    out = nc.dram_tensor("out", (TT, P, D), F32, kind="ExternalOutput").ap()
    build(nc, *aps, out)
    r = run_bass_kernel_spmd(nc, [arrays], core_ids=[0])
    return r.results[0]["out"].reshape(1, T, D)
```
